# Optimizing a Trainium2 kernel written in Bass

```python
import math
import jax, jax.numpy as jnp
from jax import lax
import numpy as np

D_MODEL = 1024
BATCH = 1
SEQ = 128
DEPTH = 1
DEC_BATCH = 1
DEC_SEQ = 512
PAST_LEN = 256

GRID_W = 64
D_MIX = D_MODEL
N_MIXERS = 4
D_GROUP = D_MIX // N_MIXERS
MLSTM_HEADS = 4
MLSTM_DH = D_GROUP // MLSTM_HEADS
MLSTM_CHUNK = 64
GMLP_GROUPS = 4
GMLP_CHUNK = 128
GMLP_DG = D_GROUP // GMLP_GROUPS
POOL_WINDOWS = (2, 4, 8, 16)
POOL_DG = D_GROUP // len(POOL_WINDOWS)
CONV_W = 3
D_FF = 2816
FFN_CONV_W = 3
N_MOD = 6
N_GATE_COLS = 4 * MLSTM_HEADS
D_IN = 4 * D_GROUP + N_GATE_COLS + 2 * D_GROUP + D_GROUP + 3 * D_GROUP
EPS = 1e-6
POS_BASE = 10000.0

kernel_name = "hybrid_mlstm_gmlp_pool_conv_dit_step"

def rms_norm(x, g):
    xf = x.astype(jnp.float32)
    y = xf * lax.rsqrt(jnp.mean(xf * xf, axis=-1, keepdims=True) + EPS)
    return (y * g.astype(jnp.float32)).astype(x.dtype)

def dwconv_centred(x, w):
    k = w.shape[0]
    p = k // 2
    t = x.shape[1]
    xp = jnp.pad(x, ((0, 0), (p, k - 1 - p), (0, 0)))
    return sum(xp[:, j:j + t] * w[j] for j in range(k))

def grid_sincos(t_len, d):
    rows = t_len // GRID_W
    r = jnp.repeat(jnp.arange(rows, dtype=jnp.float32), GRID_W)
    col = jnp.tile(jnp.arange(GRID_W, dtype=jnp.float32), rows)
    quarter = d // 4
    omega = 1.0 / (POS_BASE ** (jnp.arange(quarter, dtype=jnp.float32) / quarter))

    def emb(p):
        a = p[:, None] * omega[None, :]
        return jnp.concatenate([jnp.sin(a), jnp.cos(a)], axis=-1)

    return jnp.concatenate([emb(r), emb(col)], axis=-1)

def mlstm_chunkwise(q, k, v, ig, lf, C0, n0, m0):
    B, T, H, D = q.shape
    L = MLSTM_CHUNK
    nc = T // L

    def to_chunks(a):
        a = a.reshape((B, nc, L) + a.shape[2:])
        a = jnp.moveaxis(a, 3, 2)
        return jnp.moveaxis(a, 1, 0)

    xs = (to_chunks(q), to_chunks(k), to_chunks(v), to_chunks(ig), to_chunks(lf))
    lower = jnp.tril(jnp.ones((L, L), dtype=bool))

    def step(carry, inp):
        C, n, m = carry
        qb, kb, vb, ib, fb = inp
        b = jnp.cumsum(fb, axis=-1)
        dmat = b[..., :, None] - b[..., None, :] + ib[..., None, :]
        dmat = jnp.where(lower, dmat, -jnp.inf)
        inter = b + m[..., None]
        m_row = jnp.maximum(jnp.max(dmat, axis=-1), inter)
        w_intra = jnp.exp(dmat - m_row[..., None])
        w_inter = jnp.exp(inter - m_row)
        s = jnp.einsum('bhtd,bhsd->bhts', qb, kb) * w_intra
        num = (w_inter[..., None] * jnp.einsum('bhtd,bhde->bhte', qb, C)
               + jnp.einsum('bhts,bhse->bhte', s, vb))
        den = w_inter * jnp.einsum('bhtd,bhd->bht', qb, n) + jnp.sum(s, axis=-1)
        h = num / jnp.maximum(jnp.abs(den), jnp.exp(-m_row))[..., None]
        b_last = b[..., -1]
        wk = b_last[..., None] - b + ib
        m_new = jnp.maximum(b_last + m, jnp.max(wk, axis=-1))
        a_prev = jnp.exp(b_last + m - m_new)
        a_k = jnp.exp(wk - m_new[..., None])
        C_new = a_prev[..., None, None] * C + jnp.einsum('bhs,bhsd,bhse->bhde', a_k, kb, vb)
        n_new = a_prev[..., None] * n + jnp.einsum('bhs,bhsd->bhd', a_k, kb)
        return (C_new, n_new, m_new), h

    (C, n, m), hs = lax.scan(step, (C0, n0, m0), xs)
    h = jnp.moveaxis(hs, 0, 1)
    h = jnp.moveaxis(h, 2, 3).reshape(B, T, H, D)
    return h, C, n, m

def bi_mlstm(q, k, v, gates, st):
    C0, n0, m0 = st
    h_f, Cf, nf, mf = mlstm_chunkwise(q, k, v, gates[:, :, 0], jax.nn.log_sigmoid(gates[:, :, 1]),
                                      C0[:, 0], n0[:, 0], m0[:, 0])
    fl = lambda a: jnp.flip(a, axis=1)
    h_b, Cb, nb, mb = mlstm_chunkwise(fl(q), fl(k), fl(v), fl(gates[:, :, 2]),
                                      fl(jax.nn.log_sigmoid(gates[:, :, 3])),
                                      C0[:, 1], n0[:, 1], m0[:, 1])
    h = h_f + fl(h_b)
    return h, (jnp.stack([Cf, Cb], axis=1), jnp.stack([nf, nb], axis=1), jnp.stack([mf, mb], axis=1))

def chunk_spatial_gate(u, v, ws, bs):
    B, T, _ = u.shape
    nchunk = T // GMLP_CHUNK
    vg = v.reshape(B, nchunk, GMLP_CHUNK, GMLP_GROUPS, GMLP_DG)
    mixed = jnp.einsum('gts,bnsgc->bntgc', ws, vg) + bs.T[None, None, :, :, None]
    return u * mixed.reshape(B, T, D_GROUP).astype(u.dtype)

def multiscale_pool(z, w_pool, scale):
    B, T, _ = z.shape
    zf = z.astype(jnp.float32).reshape(B, T, len(POOL_WINDOWS), POOL_DG)
    P = jnp.concatenate([jnp.zeros((B, 1, len(POOL_WINDOWS), POOL_DG), jnp.float32),
                         jnp.cumsum(zf, axis=1)], axis=1)
    t = jnp.arange(T)
    outs = []
    for g, w in enumerate(POOL_WINDOWS):
        lo = jnp.clip(t - w // 2, 0, T)
        hi = jnp.clip(t + w // 2, 0, T)
        Pg = P[:, :, g]
        cnt = (hi - lo).astype(jnp.float32)[None, :, None]
        outs.append((Pg[:, hi] - Pg[:, lo]) / cnt - zf[:, :, g])
    pooled = jnp.stack(outs, axis=2)
    y = jnp.einsum('btgc,gcd->btgd', pooled, w_pool.astype(jnp.float32)).reshape(B, T, D_GROUP)
    return (y * scale.astype(jnp.float32)).astype(z.dtype)

def mixer_sublayer(h, st, w_in, gate_b, gmlp_ws, gmlp_b, pool_w, pool_scale, conv_w, w_out):
    B, T, _ = h.shape
    z = h @ w_in
    sizes = (D_GROUP,) * 4 + (N_GATE_COLS,) + (D_GROUP,) * 2 + (D_GROUP,) + (D_GROUP,) * 3
    idx = [int(i) for i in np.cumsum(sizes)[:-1]]
    q, k, v, o, g, gu, gv, pz, cb, cc, cx = jnp.split(z, idx, axis=-1)
    heads = lambda a: a.reshape(B, T, MLSTM_HEADS, MLSTM_DH).astype(jnp.float32)
    gates = g.reshape(B, T, 4, MLSTM_HEADS).astype(jnp.float32) + gate_b.astype(jnp.float32)
    h_a, new_st = bi_mlstm(heads(q), heads(k) * (MLSTM_DH ** -0.5), heads(v), gates, st)
    y_a = (jax.nn.sigmoid(o.astype(jnp.float32)) * h_a.reshape(B, T, D_GROUP)).astype(h.dtype)
    y_b = chunk_spatial_gate(gu, gv, gmlp_ws, gmlp_b)
    y_c = multiscale_pool(pz, pool_w, pool_scale)
    y_d = cb * dwconv_centred(cc * cx, conv_w)
    y = jnp.concatenate([y_a, y_b, y_c, y_d], axis=-1) @ w_out
    return y, new_st

def trunk_layer(x, cond, st, norm_g, ada_w, ada_b, w_in, gate_b, gmlp_ws, gmlp_b, pool_w,
                pool_scale, conv_w, w_out, ffn_up, ffn_conv, ffn_down):
    mod = (jax.nn.silu(cond) @ ada_w + ada_b).astype(x.dtype).reshape(cond.shape[0], N_MOD, 1, D_MODEL)
    sh1, sc1, gt1, sh2, sc2, gt2 = [mod[:, i] for i in range(N_MOD)]
    h = rms_norm(x, norm_g[0]) * (1 + sc1) + sh1
    y, st = mixer_sublayer(h, st, w_in, gate_b, gmlp_ws, gmlp_b, pool_w, pool_scale, conv_w, w_out)
    x = x + gt1 * rms_norm(y, norm_g[1])
    h = rms_norm(x, norm_g[2]) * (1 + sc2) + sh2
    a = dwconv_centred(h @ ffn_up, ffn_conv)
    val, gate = jnp.split(a, 2, axis=-1)
    y = (jax.nn.silu(gate) * val) @ ffn_down
    x = x + gt2 * rms_norm(y, norm_g[3])
    return x, st

def setup_inputs(seed: int = 0) -> dict:
    key = jax.random.key(seed)
    ks = jax.random.split(key, 24)
    nrm = lambda k, s: jax.random.normal(k, s, jnp.float32)
    H = MLSTM_HEADS
    fg_base = jnp.linspace(3.0, 6.0, H, dtype=jnp.float32)
    zero_h = jnp.zeros((H,), jnp.float32)
    gate_base = jnp.stack([zero_h, fg_base, zero_h, fg_base], axis=0)
    return {
        "x_prompt": nrm(ks[0], (BATCH, SEQ, D_MODEL)),
        "x_sample": nrm(ks[1], (DEC_BATCH, DEC_SEQ, D_MODEL)),
        "state_C": 0.1 * nrm(ks[2], (DEC_BATCH, DEPTH, 2, H, MLSTM_DH, MLSTM_DH)),
        "state_n": 0.1 * nrm(ks[3], (DEC_BATCH, DEPTH, 2, H, MLSTM_DH)),
        "state_m": 0.5 * nrm(ks[4], (DEC_BATCH, DEPTH, 2, H)),
        "c": nrm(ks[5], (DEC_BATCH, D_MODEL)),
        "c_ctx": nrm(ks[6], (D_MODEL,)),
        "norm_g": 1.0 + 0.1 * nrm(ks[7], (DEPTH, 4, D_MODEL)),
        "ada_w": 0.5 * D_MODEL ** -0.5 * nrm(ks[8], (DEPTH, D_MODEL, N_MOD * D_MODEL)),
        "ada_b": 0.02 * nrm(ks[9], (DEPTH, N_MOD * D_MODEL)),
        "w_in": D_MODEL ** -0.5 * nrm(ks[10], (DEPTH, D_MODEL, D_IN)),
        "gate_b": gate_base[None] + 0.1 * nrm(ks[11], (DEPTH, 4, H)),
        "gmlp_ws": GMLP_CHUNK ** -0.5 * nrm(ks[12], (DEPTH, GMLP_GROUPS, GMLP_CHUNK, GMLP_CHUNK)),
        "gmlp_b": 1.0 + 0.1 * nrm(ks[13], (DEPTH, GMLP_GROUPS, GMLP_CHUNK)),
        "pool_w": POOL_DG ** -0.5 * nrm(ks[14], (DEPTH, len(POOL_WINDOWS), POOL_DG, POOL_DG)),
        "pool_scale": 1.0 + 0.1 * nrm(ks[15], (DEPTH, D_GROUP)),
        "conv_w": CONV_W ** -0.5 * nrm(ks[16], (DEPTH, CONV_W, D_GROUP)),
        "w_out": D_MIX ** -0.5 * nrm(ks[17], (DEPTH, D_MIX, D_MODEL)),
        "ffn_up": D_MODEL ** -0.5 * nrm(ks[18], (DEPTH, D_MODEL, 2 * D_FF)),
        "ffn_conv": FFN_CONV_W ** -0.5 * nrm(ks[19], (DEPTH, FFN_CONV_W, 2 * D_FF)),
        "ffn_down": D_FF ** -0.5 * nrm(ks[20], (DEPTH, D_FF, D_MODEL)),
    }

def reference(x_prompt, x_sample, state_C, state_n, state_m, c, c_ctx, norm_g, ada_w, ada_b, w_in,
              gate_b, gmlp_ws, gmlp_b, pool_w, pool_scale, conv_w, w_out, ffn_up, ffn_conv, ffn_down):
    f32 = jnp.float32
    H, Dh = MLSTM_HEADS, MLSTM_DH

    def lw(l):
        return (norm_g[l], ada_w[l], ada_b[l], w_in[l], gate_b[l], gmlp_ws[l], gmlp_b[l], pool_w[l],
                pool_scale[l], conv_w[l], w_out[l], ffn_up[l], ffn_conv[l], ffn_down[l])

    Bp = x_prompt.shape[0]
    zero_state = (jnp.zeros((Bp, 2, H, Dh, Dh), f32), jnp.zeros((Bp, 2, H, Dh), f32),
                  jnp.zeros((Bp, 2, H), f32))
    xp = x_prompt
    Cs, ns, ms = [], [], []
    for l in range(DEPTH):
        xp, (C_l, n_l, m_l) = trunk_layer(xp, c_ctx[None, :], zero_state, *lw(l))
        Cs.append(C_l)
        ns.append(n_l)
        ms.append(m_l)

    T = x_sample.shape[1]
    xs = x_sample + grid_sincos(T, D_MODEL).astype(x_sample.dtype)[None]
    for l in range(DEPTH):
        st = (state_C[:, l].astype(f32), state_n[:, l].astype(f32), state_m[:, l].astype(f32))
        xs, _ = trunk_layer(xs, c, st, *lw(l))

    return (xp, xs, jnp.stack(Cs, axis=1), jnp.stack(ns, axis=1), jnp.stack(ms, axis=1))


_drawn_inputs = setup_inputs


def setup_inputs(seed=0):
    import zlib

    import numpy as np

    out = dict(_drawn_inputs(seed))
    spreads = {}
    factors = {'state_C': 8.0, 'state_n': 5.874, 'state_m': 8.0, 'gmlp_b': 5.192, 'pool_scale': 6.499}
    for name, (base, spread) in spreads.items():
        noise = np.random.default_rng([zlib.crc32(name.encode()), seed]).standard_normal(out[name].shape)
        drawn = base * np.exp(spread * noise) if base else spread * noise
        out[name] = __import__('jax').numpy.asarray(drawn.astype(out[name].dtype))
    for name, factor in factors.items():
        out[name] = (out[name] * factor).astype(out[name].dtype)
    return out
```

```python
from contextlib import ExitStack

import concourse.bass as bass
from concourse import mybir

F32 = mybir.dt.float32
F32R = mybir.dt.float32r
BF16 = mybir.dt.bfloat16
ALU = mybir.AluOpType
ACT = mybir.ActivationFunctionType

P = 128
D = 1024
KC = D // P
TILES = 5
TOK = TILES * P
CTX = P
HALF = TOK // 2
HEADS, DH = 4, 64
DG = 256
D_FF = 2816
FT = D_FF // P
EPS = 1e-6
NEG = -1e30
SLOT = 4 * (DG + 16)
RING = 4
AHEAD = 3

Q0, K0, V0, O0, G0, GU0, GV0, PZ0, CB0, CC0, CX0 = 0, 256, 512, 768, 1024, 1040, 1296, 1552, 1808, 2064, 2320

PADW, PC_, PS_ = 672, 8, 152
UPW = TOK + 4
AW = TOK + 2


HEAD_STEPS = [("ada", 0), ("ada", 1), ("p2", 0), ("ada", 2), ("p2", 1), ("ada", 3), ("p2", 2), ("p2", 3)]
MIX_STEPS = [
    ("q", 0), ("q", 1), ("k", 0), ("k", 1), ("v", 0), ("v", 1), ("v", 2), ("gi", 0), ("gf", 0),
    ("kt", 0), ("kt", 1), ("gv", 0), ("gv", 1), ("mx", 0), ("mx", 1), ("gu", 0), ("ct", 0),
    ("B", 0), ("gu", 1), ("C", 0), ("B", 1), ("cc", 0), ("C", 1), ("B", 2), ("cx", 0), ("C", 2),
    ("B", 3), ("cb", 0), ("C", 3), ("B", 4), ("cc", 1), ("C", 4), ("B", 5), ("cx", 1), ("C", 5),
    ("B", 6), ("cb", 1), ("C", 6), ("B", 7), ("pz", 0), ("C", 7), ("B", 8), ("ada", 4), ("pl", 0), ("C", 8),
    ("B", 9), ("pz", 1), ("p2", 4), ("C", 9), ("ada", 5), ("pl", 1), ("ada", 6), ("p2", 5),
    ("o", 0), ("p2", 6), ("o", 1), ("ada", 7), ("ada", 8), ("p2", 7), ("ada", 9), ("p2", 8), ("p2", 9)]
PLAN = HEAD_STEPS + MIX_STEPS
FEATURE = {"q": Q0, "k": K0, "o": O0, "gu": GU0, "pz": PZ0, "cb": CB0, "cc": CC0, "cx": CX0}
MUNITS = [(0, 0), (0, 1), (1, 0), (2, 0), (3, 0), (4, 0), (4, 1), (3, 1), (2, 1), (1, 1)]
OUT_ORDER = [6, 2, 7, 3, 4, 5, 0, 1]
PASS_TILES = [(0, 1, 2), (3, 4)]
PASS_PAIR = {0: 0, 1: 1, 2: 2, 3: 3, 4: 0}
PLAN_OUT = ([("k", 0, n) for n in range(KC)]
            + [("k", 1, 0), ("epi", 0), ("k", 1, 1), ("epi", 1), ("k", 1, 2), ("epi", 2), ("k", 1, 3),
               ("nrm", 0), ("k", 1, 4), ("tr", 0), ("nrm", 1), ("k", 1, 5), ("tr", 1), ("nrm", 2),
               ("k", 1, 6), ("k", 1, 7), ("tr", 2), ("epi", 3), ("epi", 4), ("ada", 10), ("nrm", 3),
               ("tr", 3), ("p2", 10), ("nrm", 4), ("ada", 11), ("tr", 4), ("p2", 11)])
OUT_PAIR = {("tr", 0): 1, ("tr", 1): 2, ("tr", 2): 1, ("tr", 3): 2, ("tr", 4): 1,
            ("ada", 10): 3, ("ada", 11): 3, ("p2", 10): 0, ("p2", 11): 2}
PLAN_DOWN = ([("k", 0, n) for n in range(FT)]
             + [("k", 1, 0), ("epi", 0), ("k", 1, 1), ("epi", 1), ("k", 1, 2), ("epi", 2)]
             + [("k", 1, n) for n in range(3, FT)] + [("epi", 3), ("epi", 4)])


def plan_units():
    units, upto = [], {}
    done_v = done_gv = False
    for s in PLAN:
        if s[0] == "ada":
            units += [("ada", s[1], q) for q in range(4)]
        elif s[0] in FEATURE:
            units.append(("ft", FEATURE[s[0]] + P * s[1]))
        elif s[0] == "v" and not done_v:
            units += [("vg", 0), ("vg", 1)]
            done_v = True
        elif s[0] == "gv" and not done_gv:
            units += [("gv", 0), ("gv", 1)]
            done_gv = True
        upto[s] = len(units)
    for s in PLAN_OUT:
        if s[0] == "k":
            units.append(("out", OUT_ORDER[s[2]]))
        elif s[0] == "ada":
            units += [("ada", s[1], q) for q in range(4)]
        upto[("out",) + s] = len(units)
    up0 = len(units)
    units += [("up", n) for n in range(2 * FT)]
    for s in PLAN_DOWN:
        if s[0] == "k":
            units.append(("down", s[2]))
        upto[("down",) + s] = len(units)
    return units, upto, up0


def plan_pairs(loops):
    readers = {"v": 2, "gf": 2, "ct": 2, "tr": 2}
    nfilled, ndrained, out = [0] * 4, [0] * 4, {}

    def use(key, pair, n):
        out[key] = (pair, nfilled[pair] + 1, ndrained[pair], ndrained[pair] + n)
        nfilled[pair] += 1
        ndrained[pair] += n

    use("consts", 3, 1)
    for g in range(TILES):
        use(("xt", g), 2 + g % 2, 1)
    turn = 0
    for s in PLAN:
        if s[0] in "BC":
            continue
        use(s, turn % 2, readers.get(s[0], 1))
        turn += 1
    for stage, plan in (("out", PLAN_OUT), ("down", PLAN_DOWN)):
        if stage == "down":
            for pair in range(4):
                out[("up", pair)] = (pair, nfilled[pair] + 1, ndrained[pair], ndrained[pair] + 1)
                nfilled[pair] += loops
                ndrained[pair] += loops
        for s in plan:
            if s[0] == "k" and s[2] == 0:
                for g in PASS_TILES[s[1]]:
                    use((stage, "epi", g), PASS_PAIR[g], 1)
            elif s[0] in ("tr", "ada", "p2"):
                use((stage,) + s, OUT_PAIR[s], readers.get(s[0], 1))
    return out


def hybrid_trunk_layer(nc, x_prompt, x_sample, state_C, state_n, state_m, c, c_ctx, norm_g, ada_w, ada_b, w_in,
                       gate_b, gmlp_ws, gmlp_b, pool_w, pool_scale, conv_w, w_out, ffn_up, ffn_conv, ffn_down,
                       pos_row, pos_col, pool_edge, y_prompt, y_sample, new_C, new_n, new_m):
    LOOPS = 2 * FT // RING
    assert LOOPS * RING == 2 * FT
    UNITS, UPTO, UP0 = plan_units()
    assert UP0 % RING == 0
    USE = plan_pairs(LOOPS)
    NU = len(UNITS)
    NCONST = 16 * 15
    POOL_IN = 16 * 14
    made_all = 25

    ada_v = ada_w[0].rearrange("(p c) n -> p c n", c=KC)
    win_v = w_in[0].rearrange("(c p) n -> p c n", p=P)
    wout_v = w_out[0].rearrange("(c p) n -> p c n", p=P)
    up_v = ffn_up[0].rearrange("(c p) n -> p c n", p=P)
    down_v = ffn_down[0].rearrange("(c p) n -> p c n", p=P)
    x_tile = [x_prompt[0]] + [x_sample[0, P * i:P * i + P, :] for i in range(TILES - 1)]
    y_tile = [y_prompt[0]] + [y_sample[0, P * i:P * i + P, :] for i in range(TILES - 1)]

    with ExitStack() as ctx:
        sbuf_end = nc.sbuf_usable_end
        place = {"at": (nc.sbuf_base + 31) // 32 * 32}

        def at(name, shape, dt, offset):
            size = 1
            for n in shape[1:]:
                size *= n
            size *= 2 if dt == BF16 else 4
            assert offset + size <= sbuf_end, (name, offset + size - sbuf_end)
            return nc.alloc_sbuf_tensor_at(name, shape, dt, offset=offset), offset + size

        def sb(name, shape, dt=F32):
            t, end = at(name, shape, dt, place["at"])
            place["at"] = (end + 31) // 32 * 32
            return t

        def sem(name):
            return ctx.enter_context(nc.semaphore(name))

        Hhi = sb("Hhi", [P, KC, TOK], F32R)
        Hlo = sb("Hlo", [P, KC, TOK], F32R)
        GATE = sb("GATE", [P, 2, D])
        RAW = sb("RAW", [P, RING, SLOT])
        WHI = sb("WHI", [P, RING, SLOT], F32R)
        WLO = sb("WLO", [P, RING, SLOT], F32R)
        JUNK = sb("JUNK", [P, D], BF16)
        MODROW = sb("MODROW", [4, 512])
        SELG = sb("SELG", [4, 2, P])
        IDENT = sb("IDENT", [P, P])
        ONES = sb("ONES", [P, P])
        MODC = sb("MODC", [P, 6 * KC, 2])
        BCOL = sb("BCOL", [P, 6 * KC])
        SCOL = sb("SCOL", [P, 44])
        FW = sb("FW", [P, 3, 2 * FT])
        AMOD = sb("AMOD", [P, 2, 2, KC])
        STAT = sb("STAT", [P, 4, 3, TILES])
        EPSC = sb("EPSC", [P, 1])
        SCND = sb("SCND", [P, 4 * KC + P - 4], F32R)
        region = place["at"]

        Y = sb("Y", [P, KC, TOK])
        QK = sb("QK", [P, 4, TOK])
        BG = sb("BG", [P, 2, 512])
        KT = sb("KT", [P, TILES, DG])
        V = sb("V", [P, TILES, DG])
        GV = sb("GV", [P, TILES, DG])
        WST = sb("WST", [P, 4, P])
        HA = sb("HA", [P, 2, TOK])
        SA = sb("SA", [P, 2, PADW])
        SBb = sb("SBb", [P, PADW])
        SCb = sb("SCb", [P, PADW])
        XE = sb("XE", [P, 4, P])
        SS = sb("SS", [P, 4, P])
        WE = sb("WE", [P, 2, 2, P])
        QW = sb("QW", [P, 2, P])
        KW = sb("KW", [P, DG])
        CST = sb("CST", [P, 2, 2, 2, P])
        LF = sb("LF", [64, TOK])
        BR = sb("BR", [64, TOK])
        AR = sb("AR", [64, TOK])
        NM = sb("NM", [64, TOK])
        WR = sb("WR", [64, TILES, 2, P])
        COLS = sb("COLS", [P, TILES, 2, 64])
        MASK = sb("MASK", [P, 2, P])
        SELP = sb("SELP", [64, 4, P])
        PWB = sb("PWB", [P, 2, P])
        EDGE = sb("EDGE", [P, 34])
        GB = sb("GB", [P, 16])
        M0 = sb("M0", [64, 1])
        MS = sb("MS", [64, 1])
        NS = sb("NS", [P, 2, 2])
        CND = sb("CND", [P, 2, KC])
        print("first sub-layer ends", place["at"], "of", sbuf_end)

        base = {}
        cur = region
        for name, size in (("Y", KC * TOK * 4), ("QK", 4 * TOK * 4), ("BG", 4096), ("KT", 5120), ("V", 5120),
                           ("GV", 5120), ("WST", 2048), ("HA", 5120), ("SA", 2 * PADW * 4), ("SBb", PADW * 4),
                           ("SCb", PADW * 4), ("XE", 2048), ("SS", 2048)):
            base[name] = cur
            cur += size
        POSC, _ = at("POSC", [P, 512], F32, base["QK"])
        POSR, _ = at("POSR", [P, 4, 512], F32, base["QK"] + 2048)
        XN, _ = at("XN", [P, 2, D], F32, base["KT"])
        SMALL, _ = at("SMALL", [44, P], F32, base["GV"])
        BROWS, _ = at("BROWS", [48, P], F32, base["GV"] + 512)
        FROWS, _ = at("FROWS", [44, 3, P], F32, base["GV"] + 1024)
        BSB, _ = at("BSB", [P, 2, P], F32, base["BG"])
        CSO, _ = at("CSO", [P, 2, 2, DH], F32, base["Y"])
        BIG1, _ = at("BIG1", [36, TOK - CTX], F32, base["SA"] + 3072)
        WS, _ = at("WS", [P, 4, P], F32, base["GV"] + 2560)
        XS, _ = at("XS", [P, 2, D], F32, base["HA"])
        G2, _ = at("G2", [P, TILES, 2, 64], F32, base["SBb"])
        TMP, _ = at("TMP", [P, TOK], F32, base["SCb"])

        r0 = region
        ACTF, r1 = at("ACTF", [P, FT, AW], F32, r0)
        r1 = (r1 + 31) // 32 * 32
        X2, r2 = at("X2", [P, TILES, D], F32, r1)
        ASHI, r3 = at("ASHI", [P, 3, 392], F32R, r2)
        ASLO, _ = at("ASLO", [P, 3, 392], F32R, r3)
        UP, r4 = at("UP", [P, 2, 2, UPW], F32, r2)
        r4 = (r4 + 31) // 32 * 32
        CV, r5 = at("CV", [P, 2, 2, AW], F32, r4)
        T2, _ = at("T2", [P, D], F32, r4)
        HT2, _ = at("HT2", [P, KC, P], F32, r4 + 4096)
        r5 = (r5 + 31) // 32 * 32
        XN2, r6 = at("XN2", [P, D], F32, r5)

        PAIR = [ctx.enter_context(nc.psum_tensor(f"PAIR{i}", [P, 2 * 512], F32)) for i in range(4)]
        psQ, psM = PAIR[2][:, 0:512], PAIR[2][:, 512:1024]
        psW, psN = PAIR[3][:, 0:512], PAIR[3][:, 512:1024]

        raw_in = [sem(f"raw_in{i}") for i in range(RING)]
        hi_split, lo_split = sem("hi_split"), sem("lo_split")
        ada_used, chunk_used = sem("ada_used"), sem("chunk_used")
        filled = [sem(f"filled{i}") for i in range(4)]
        drained = [sem(f"drained{i}") for i in range(4)]
        consts_in, pool_in, pos_in = sem("consts_in"), sem("pool_in"), sem("pos_in")
        x_in = [sem(f"x_in{i}") for i in range(2)]
        pool_made = sem("pool_made")
        vlink, alink = sem("vlink"), sem("alink")
        cond_silu, cond_split, n0_set = sem("cond_silu"), sem("cond_split"), sem("n0_set")
        x_pos, x_sq, x_root, x_normed = sem("x_pos"), sem("x_sq"), sem("x_root"), sem("x_normed")
        mod1, mod2, h_hi, h_lo = sem("mod1"), sem("mod2"), sem("h_hi"), sem("h_lo")
        softplus, rows_ready = sem("softplus"), sem("rows_ready")
        psQ_even, psQ_full = sem("psQ_even"), sem("psQ_full")
        psM_full, psW_full = sem("psM_full"), sem("psW_full")
        psN_full, psC_full = sem("psN_full"), sem("psC_full")
        xe_ready, e_ready, we_ready = sem("xe_ready"), sem("e_ready"), sem("we_ready")
        s_ready, qw_ready, kw_ready = sem("s_ready"), sem("qw_ready"), sem("kw_ready")
        n_read, c_read, states_out = sem("n_read"), sem("c_read"), sem("states_out")
        pads_zero, conv_done, pooled = sem("pads_zero"), sem("conv_done"), sem("pooled")
        y_made, bg_in, bg_used = sem("y_made"), sem("bg_in"), sem("bg_used")
        x2_in, act_hi, act_lo = sem("x2_in"), sem("act_hi"), sem("act_lo")
        y_sq, y_root, x2_new = sem("y_sq"), sem("y_root"), sem("x2_new")
        n_sq, n_root, n_xn, n_lo = sem("n_sq"), sem("n_root"), sem("n_xn"), sem("n_lo")
        up_free, silu_out, ff_out, y_out = sem("up_free"), sem("silu_out"), sem("ff_out"), sem("y_out")

        block = ctx.enter_context(nc.Block())

        m_index = {u: n for n, u in enumerate(MUNITS)}
        UPD = [u for u in MUNITS if u not in ((4, 0), (1, 1))]
        CARRY = [u for u in MUNITS if u[0] > 0]

        def halves(t):
            return t[:, :].rearrange("p (h n) -> p h n", h=2)[:, :, 0:HALF]

        def pieces(o_ctx, o_smp):
            a = HALF - CTX
            return [(0, CTX, o_ctx), (CTX, HALF, o_smp), (512, 512 + HALF, o_smp + a)]

        def cols(g):
            return slice(P * g, P * g + P)

        def wait_filled(eng, key):
            eng.wait_ge(filled[USE[key][0]], USE[key][1])
            return PAIR[USE[key][0]]

        def wait_free(eng, key):
            if USE[key][2]:
                eng.wait_ge(drained[USE[key][0]], USE[key][2])
            return PAIR[USE[key][0]]

        def wait_first_reader(eng, key):
            eng.wait_ge(drained[USE[key][0]], USE[key][2] + 1)

        def wait_copied(eng, key):
            eng.wait_ge(drained[USE[key][0]], USE[key][3])

        def raw_count(n):
            return 16 * sum(2 if UNITS[m][0] == "vg" else 1 for m in range(n % RING, n + 1, RING))

        def width(n):
            return SLOT if UNITS[n][0] == "vg" else D

        ALL = [("", s) for s in PLAN] + [("out", s) for s in PLAN_OUT] + [("up", None)] + [("down", s) for s in PLAN_DOWN]
        release, goal, n_ada, n_chunk, pos = {}, {}, 0, 0, 0
        for at_, (stage, s) in enumerate(ALL):
            key = s if stage == "" else (stage,) + (s or ())
            if stage == "up":
                for n in range(2 * FT):
                    pair, f, _, _ = USE[("up", n % 4)]
                    release[UP0 + n] = (filled[pair], f + n // 4, at_, False)
                pos = UP0 + 2 * FT
                goal[at_] = pos
                continue
            end = UPTO[key]
            if s[0] == "ada":
                for q in range(3):
                    n_ada += 1
                    release[pos + q] = (ada_used, n_ada, at_, True)
                release[pos + 3] = (filled[USE[key][0]], USE[key][1], at_, False)
            elif s[0] == "k" and stage:
                last_k = (KC if stage == "out" else FT) - 1
                if s[2] < last_k:
                    n_chunk += 1
                    release[pos] = (chunk_used, n_chunk, at_, False)
                else:
                    u = USE[(stage, "epi", PASS_TILES[s[1]][-1])]
                    release[pos] = (filled[u[0]], u[1], at_, False)
            elif s in (("v", 2), ("gv", 1)):
                for q in (1, 2):
                    release[pos - q] = (filled[USE[key][0]], USE[key][1], at_, False)
            elif not stage and s[0] in FEATURE:
                release[pos] = (filled[USE[key][0]], USE[key][1], at_, False)
            pos = end
        for at_, (stage, s) in enumerate(ALL):
            if stage == "up":
                continue
            key = s if stage == "" else (stage,) + s
            n = UPTO[key]
            while n < NU and n < UPTO[key] + AHEAD:
                r = release.get(n - RING)
                if r is not None and r[2] >= at_:
                    break
                n += 1
            goal[at_] = n
        UP_STEP = len(PLAN) + len(PLAN_OUT)
        goal[UP_STEP - 1] = UP0 + AHEAD

        def wait_slot(eng, n):
            if n >= RING:
                eng.wait_ge(release[n - RING][0], release[n - RING][1])

        CHUNKS = [("out", s) for s in PLAN_OUT if s[0] == "k"] + [("down", s) for s in PLAN_DOWN if s[0] == "k"]
        chunk_unit = [UPTO[(st,) + s] - 1 for st, s in CHUNKS]
        chunk_at = {(st,) + s: n for n, (st, s) in enumerate(CHUNKS)}

        def chunk_source(n):
            stage, (_, half, k) = CHUNKS[n]
            if stage == "out":
                a, b = ((0, 3 * P), (3 * P, TOK))[half]
                return Y[:, OUT_ORDER[k], a:b], b - a
            a, b = ((0, 3 * P + 2), (3 * P + 2, AW))[half]
            return ACTF[:, k, a:b], b - a

        def chunk_limit(n):
            return min(n + 3, len(CHUNKS), 2 * KC if CHUNKS[n][0] == "out" else len(CHUNKS))

        def wait_chunk_slot(eng, n):
            if n >= 3:
                r = release[chunk_unit[n - 3]]
                eng.wait_ge(r[0], r[1])

        @block.sync
        def _(sp):
            def source(u):
                if u[0] == "ada":
                    _, p, q = u
                    return [(0, 2, 512, ada_v[:, 2 * q:2 * q + 2, 512 * p:512 * p + 512])]
                if u[0] == "ft":
                    return [(0, KC, P, win_v[:, :, u[1]:u[1] + P])]
                if u[0] == "vg":
                    q = u[1]
                    return [(0, 4, DG, win_v[:, 4 * q:4 * q + 4, V0:V0 + DG]),
                            (DG, 4, 16, win_v[:, 4 * q:4 * q + 4, G0:G0 + 16])]
                if u[0] == "gv":
                    return [(0, 4, DG, win_v[:, 4 * u[1]:4 * u[1] + 4, GV0:GV0 + DG])]
                return [(0, 1, D, (wout_v if u[0] == "out" else down_v)[:, u[1]:u[1] + 1, :])]

            def load(n):
                if n >= RING:
                    sp.wait_ge(hi_split, n - RING + 1)
                    sp.wait_ge(lo_split, n - RING + 1)
                slot = RAW[:, n % RING, :]
                for o, a, b, src in source(UNITS[n]):
                    if UNITS[n][0] == "vg":
                        dst = slot.rearrange("p (a b) -> p a b", a=4)[:, :, o:o + b]
                    else:
                        dst = slot[:, 0:a * b].rearrange("p (a b) -> p a b", a=a)
                    sp.dma_start(dst, src).then_inc(raw_in[n % RING], 16)

            for n in range(UP0):
                load(n)
            with sp.Fori(0, LOOPS) as i:
                for s in range(RING):
                    sp.wait_ge(hi_split, i * RING + (UP0 + s - RING + 1))
                    sp.wait_ge(lo_split, i * RING + (UP0 + s - RING + 1))
                    col = i * (2 * P) + ((s // 2) * P + (s % 2) * D_FF)
                    sp.dma_start(RAW[:, s, 0:D].rearrange("p (a b) -> p a b", a=KC),
                                 up_v[:, :, bass.ds(col, P)]).then_inc(raw_in[s], 16)
            for n in range(UP0 + 2 * FT, NU):
                load(n)
            for g in range(TILES):
                sp.wait_ge(x2_new, TILES + g + 1)
                sp.dma_start(y_tile[g], X2[:, g, :]).then_inc(y_out, 16)
            sp.wait_ge(y_out, 16 * TILES)
            sp.wait_ge(states_out, 16 * 8)

        @block.gpsimd
        def _(pool):
            made = [0]

            def make(ins):
                made[0] += 1
                ins.then_inc(pool_made, 1)
                pool.wait_ge(pool_made, made[0])

            make(pool.memset(IDENT[:, :], 0.0))
            make(pool.affine_select(out=IDENT[:, :], in_=IDENT[:, :], compare_op=ALU.not_equal, fill=1.0, base=0,
                                    pattern=[[-1, P]], channel_multiplier=1))
            make(pool.memset(ONES[:, :], 1.0))
            make(pool.memset(EPSC[:, :], EPS))
            make(pool.memset(SELG[:, :, :], 1.0))
            make(pool.affine_select(out=SELG[:, :, :], in_=SELG[:, :, :], compare_op=ALU.is_ge, fill=0.0, base=0,
                                    pattern=[[-2, 2], [0, P]], channel_multiplier=1))
            make(pool.affine_select(out=SELG[:, :, :], in_=SELG[:, :, :], compare_op=ALU.is_ge, fill=0.0, base=1,
                                    pattern=[[2, 2], [0, P]], channel_multiplier=-1))
            make(pool.memset(MASK[:, :, :], 0.0))
            make(pool.affine_select(out=MASK[:, 0, :], in_=MASK[:, 0, :], compare_op=ALU.is_ge, fill=NEG, base=0,
                                    pattern=[[1, P]], channel_multiplier=-1))
            make(pool.affine_select(out=MASK[:, 1, :], in_=MASK[:, 1, :], compare_op=ALU.is_ge, fill=NEG, base=0,
                                    pattern=[[-1, P]], channel_multiplier=1))
            for d in range(2):
                for h in range(HEADS):
                    o = DH * (h % 2)
                    r = 32 * d + h
                    make(pool.tensor_copy(SELP[:, 2 * d + h // 2, o:o + DH], IDENT[0:64, r:r + 1].to_broadcast([64, DH])))
            make(pool.memset(M0[:, :], 0.0))
            make(pool.memset(BR[:, :], 0.0))
            make(pool.memset(WR[:, :, :, :], 0.0))
            make(pool.memset(MS[:, :], 0.0))
            make(pool.memset(CST[:, :, :, :, :], 0.0))
            make(pool.memset(PWB[:, :, :], 0.0))
            make(pool.memset(BIG1[:, :], 1.0))
            assert made[0] == made_all
            for d in range(2):
                pool.dma_start(M0[32 * d:32 * d + 4, :], state_m[0, 0, d].unsqueeze(1)).then_inc(pool_in, 16)
                for h in range(HEADS):
                    o = DH * (h % 2)
                    pool.dma_start(CST[o:o + DH, d, h // 2, 0, o:o + DH], state_C[0, 0, d, h]).then_inc(pool_in, 16)
            for w in range(4):
                o = DH * (w % 2)
                pool.dma_start(PWB[o:o + DH, w // 2, o:o + DH], pool_w[0, w]).then_inc(pool_in, 16)

            def gate_rows(n, p):
                if n:
                    pool.wait_ge(bg_used, n)
                col = 512 * (p % 2)
                pool.dma_start(BG[:, 0, :], norm_g[0, 1 if p < 6 else 3, col:col + 512].partition_broadcast(P))\
                    .then_inc(bg_in, 16)
                pool.dma_start(BG[:, 1, :], ada_b[0, 512 * p:512 * p + 512].partition_broadcast(P)).then_inc(bg_in, 16)

            wait_copied(pool, ("mx", 1))
            gate_rows(0, 4)
            wait_copied(pool, ("ct", 0))
            wait_copied(pool, ("kt", 0))
            wait_copied(pool, ("kt", 1))
            for n, (g, d) in enumerate(UPD):
                if n:
                    pool.wait_ge(psC_full, n)
                w = COLS[:, g, 1, 32 * d:32 * d + HEADS].unsqueeze(2).to_broadcast([P, HEADS, DH])
                pool.tensor_tensor(KW[:, :].rearrange("p (h e) -> p h e", h=HEADS),
                                   KT[:, g, :].rearrange("p (h e) -> p h e", h=HEADS), w, ALU.mult)\
                    .then_inc(kw_ready, 1)
            gate_rows(1, 5)
            gate_rows(2, 10)
            gate_rows(3, 11)

        @block.scalar
        def _(act):
            n_link = [0]

            def link(ins):
                n_link[0] += 1
                ins.then_inc(alink, 1)
                act.wait_ge(alink, n_link[0])

            def load_x(g):
                act.dma_start(XS[:, g % 2, :], x_tile[g]).then_inc(x_in[g % 2], 16)

            def load_pos():
                for n in range(2):
                    act.dma_start(POSC[64 * n:64 * n + 64, :], pos_col).then_inc(pos_in, 16)
                    act.dma_start(POSR[64 * n:64 * n + 64, :, :], pos_row[n].partition_broadcast(64))\
                        .then_inc(pos_in, 16)

            act.dma_start(CND[:, 0, :], c_ctx.rearrange("(p c) -> p c", c=KC)).then_inc(consts_in, 16)
            act.dma_start(CND[:, 1, :], c[0].rearrange("(p c) -> p c", c=KC)).then_inc(consts_in, 16)
            load_x(0)
            load_x(1)
            load_pos()
            loads = [(SMALL[0:32, :], norm_g[0].rearrange("a (b n) -> (a b) n", n=P)),
                     (SMALL[32:38, :], conv_w[0].rearrange("a (b n) -> (a b) n", n=P)),
                     (SMALL[38:40, :], pool_scale[0].rearrange("(b n) -> b n", n=P)),
                     (SMALL[40:44, :], state_n[0, 0].rearrange("d (j h) e -> (d j) (h e)", h=2)),
                     (BROWS[:, :], ada_b[0].rearrange("(b n) -> b n", n=P)),
                     (FROWS[:, :, :], ffn_conv[0].rearrange("k (b n) -> b k n", n=P)),
                     (WS[:, :, :], gmlp_ws[0].rearrange("g t s -> t g s")),
                     (EDGE[:, :], pool_edge),
                     (GB[:, :], gate_b[0].rearrange("a h -> (a h)").partition_broadcast(P))]
            for w in range(4):
                loads.append((BSB[DH * (w % 2):DH * (w % 2) + DH, w // 2, :], gmlp_b[0, w].partition_broadcast(DH)))
            for dst, src in loads:
                act.dma_start(dst, src).then_inc(consts_in, 16)

            act.wait_ge(consts_in, NCONST)
            act.activation(CND[:, :, :], CND[:, :, :], ACT.Silu).then_inc(cond_silu, 1)

            split = [0]

            def split_to(n):
                while split[0] < n:
                    u = split[0]
                    act.wait_ge(raw_in[u % RING], raw_count(u))
                    wait_slot(act, u)
                    act.activation(WHI[:, u % RING, 0:width(u)], RAW[:, u % RING, 0:width(u)], ACT.Copy)\
                        .then_inc(hi_split, 1)
                    split[0] += 1

            for g in range(TILES):
                if g == 0:
                    act.wait_ge(x_in[0], 16)
                    act.wait_ge(pool_made, 4)
                else:
                    act.wait_ge(x_pos, g)
                act.activation(JUNK[:, :], XS[:, g % 2, :], ACT.Square, accum_out=STAT[:, 0, 0, g:g + 1])\
                    .then_inc(x_sq, 1)
                act.wait_ge(x_sq, g + 1)
                act.activation(STAT[:, 0, 1, g:g + 1], STAT[:, 0, 0, g:g + 1], ACT.Sqrt, bias=EPSC[:, :],
                               scale=1.0 / D).then_inc(x_root, 1)
                split_to(min(g + 1, RING))
                if g + 2 < TILES:
                    act.wait_ge(x_normed, g + 1)
                    load_x(g + 2)

            def scaled_copy(dst, src, sub, group, k):
                return act.activation(dst, src, ACT.Identity, scale=AMOD[:, sub, group, k:k + 1],
                                      bias=MODC[:, (24 * sub) + k, group:group + 1])

            def mix(s):
                kind, n = s
                if kind in ("q", "k"):
                    t = wait_filled(act, s)
                    i = 2 * (kind == "k") + n
                    if i == 0:
                        act.wait_ge(x_normed, TILES)
                    act.activation(QK[:, i, :].rearrange("p (h n) -> p h n", h=2), halves(t), ACT.Copy,
                                   scale=DH ** -0.5 if kind == "k" else 1.0).then_inc(drained[USE[s][0]], 1)
                elif kind == "v":
                    t = wait_filled(act, s)
                    g0, g1 = 2 * n, min(2 * n + 2, TILES)
                    act.activation(V[:, g0:g1, :], t[:, :].rearrange("p (g n) -> p g n", g=2)[:, 0:g1 - g0, 0:DG],
                                   ACT.Copy).then_inc(drained[USE[s][0]], 1)
                elif kind == "gi":
                    t = wait_filled(act, s)
                    act.activation(AR[:, :], t[0:64, 0:TOK], ACT.Copy).then_inc(drained[USE[s][0]], 1)
                elif kind == "gf":
                    t = wait_filled(act, s)
                    act.activation(LF[:, :], t[0:64, 0:TOK], ACT.Abs).then_inc(drained[USE[s][0]], 1)
                    wait_first_reader(act, s)
                    link(act.activation(LF[:, :], LF[:, :], ACT.Exp, scale=-1.0))
                    act.activation(LF[:, :], LF[:, :], ACT.Ln, bias=ONES[0:64, 0:1]).then_inc(softplus, 1)
                elif kind in ("kt", "gv"):
                    t = wait_filled(act, s)
                    g0, g1 = (0, 4) if n == 0 else (4, 5)
                    act.activation((KT if kind == "kt" else GV)[:, g0:g1, :],
                                   t[:, 0:DG * (g1 - g0)].rearrange("p (g n) -> p g n", n=DG),
                                   ACT.Copy).then_inc(drained[USE[s][0]], 1)
                elif kind == "ct":
                    t = wait_filled(act, s)
                    act.activation(COLS[:, :, 1, :], t[:, 0:TOK].rearrange("p (g k n) -> p g k n", g=TILES, k=2)[:, :, 1, :],
                                   ACT.Exp).then_inc(drained[USE[s][0]], 1)
                elif kind == "B":
                    g, d = MUNITS[n]
                    act.wait_ge(psW_full, n + 1)
                    if n:
                        act.wait_ge(n_read, n)
                        act.wait_ge(c_read, len([u for u in UPD if m_index[u] < n]))
                    act.activation(WE[:, :, :, :], psW.rearrange("p (j k n) -> p j k n", j=2, k=2), ACT.Exp)\
                        .then_inc(we_ready, 1)
                    act.wait_ge(xe_ready, n + 1)
                    act.activation(XE[:, :, :], XE[:, :, :], ACT.Exp).then_inc(e_ready, 1)
                elif kind == "C" and n == 2:
                    act.wait_ge(c_read, 2)
                    for d in range(2):
                        act.dma_start(new_C[0, 0, d].rearrange("(j h) d e -> (h d) j e", h=2), CSO[:, d, :, :])\
                            .then_inc(states_out, 16)
                        for j in range(2):
                            act.dma_start(new_n[0, 0, d, 2 * j:2 * j + 2, :].rearrange("h e -> (h e)").unsqueeze(1),
                                          NS[:, d, j:j + 1]).then_inc(states_out, 16)
                        act.dma_start(new_m[0, 0, d].unsqueeze(1), MS[32 * d:32 * d + 4, :]).then_inc(states_out, 16)
                elif kind in ("cc", "pz"):
                    t = wait_filled(act, s)
                    act.wait_ge(pads_zero, 1)
                    if n:
                        if kind == "cc":
                            act.wait_ge(conv_done, 1)
                        else:
                            wait_filled(act, ("pl", 0))
                    for a, b, o in pieces(PC_, PS_):
                        last = act.activation(SA[:, int(kind == "pz"), o:o + b - a], t[:, a:b], ACT.Copy)
                    last.then_inc(drained[USE[s][0]], 1)
                elif kind == "pl":
                    t = wait_filled(act, s)
                    for a, b, o in ((0, CTX, 0), (512, 1024, CTX)):
                        last = act.activation(Y[:, 4 + n, o:o + b - a], t[:, a:b], ACT.Copy,
                                              scale=SCOL[:, 38 + n:39 + n])
                    last.then_inc(drained[USE[s][0]], 1)
                elif kind == "o":
                    t = wait_filled(act, s)
                    if n:
                        act.wait_ge(y_made, 1)
                    act.activation(TMP[:, :].rearrange("p (h n) -> p h n", h=2), halves(t), ACT.Sigmoid)\
                        .then_inc(drained[USE[s][0]], 1)

            for at_, s in enumerate(PLAN):
                if at_ == len(HEAD_STEPS):
                    act.wait_ge(mod1, 1)
                    for k in range(KC):
                        scaled_copy(Hhi[:, k, 0:CTX], Y[:, k, 0:CTX], 0, 0, k)
                        scaled_copy(Hhi[:, k, CTX:TOK], Y[:, k, CTX:TOK], 0, 1, k).then_inc(h_hi, 1)
                split_to(goal[at_])
                mix(s)

            n_chunk_hi = [0]

            def chunks_to(n):
                while n_chunk_hi[0] < n:
                    m = n_chunk_hi[0]
                    src, w = chunk_source(m)
                    stage, (_, half, k) = CHUNKS[m]
                    if stage == "out" and half == 0:
                        y = OUT_ORDER[k]
                        if y < 2:
                            act.wait_ge(y_made, y + 1)
                        else:
                            wait_copied(act, ({1: "gu", 2: "pl", 3: "cb"}[y // 2], y % 2))
                    wait_chunk_slot(act, m)
                    act.activation(ASHI[:, m % 3, 0:w], src, ACT.Copy).then_inc(act_hi, 1)
                    n_chunk_hi[0] += 1

            def epilogue(stage, g):
                n = TILES * (stage == "down") + g
                t = wait_filled(act, (stage, "epi", g))
                i = 1 + 2 * (stage == "down")
                act.activation(JUNK[:, :], t[:, :], ACT.Square, accum_out=STAT[:, i, 0, g:g + 1]).then_inc(y_sq, 1)
                act.wait_ge(y_sq, n + 1)
                act.activation(STAT[:, i, 1, g:g + 1], STAT[:, i, 0, g:g + 1], ACT.Sqrt, bias=EPSC[:, :],
                               scale=1.0 / D).then_inc(y_root, 1)

            act.wait_ge(y_made, 2)
            for g in range(TILES):
                act.dma_start(X2[:, g, :], x_tile[g]).then_inc(x2_in, 16)
            load_pos()
            for at_, s in enumerate(PLAN_OUT, len(PLAN)):
                split_to(goal[at_])
                if s[0] == "k":
                    chunks_to(chunk_limit(chunk_at[("out",) + s]))
                elif s[0] == "epi":
                    epilogue("out", s[1])
                elif s[0] == "nrm":
                    g = s[1]
                    act.wait_ge(x2_new, g + 1)
                    act.activation(JUNK[:, :], X2[:, g, :], ACT.Square, accum_out=STAT[:, 2, 0, g:g + 1])\
                        .then_inc(n_sq, 1)
                    act.wait_ge(n_sq, g + 1)
                    act.activation(STAT[:, 2, 1, g:g + 1], STAT[:, 2, 0, g:g + 1], ACT.Sqrt, bias=EPSC[:, :],
                                   scale=1.0 / D).then_inc(n_root, 1)
                elif s[0] == "tr":
                    g = s[1]
                    t = wait_filled(act, ("out",) + s)
                    if g == 0:
                        act.wait_ge(mod2, 1)
                    for k in range(KC):
                        last = scaled_copy(Hhi[:, k, cols(g)], t[:, cols(k)], 1, int(g > 0), k)
                    last.then_inc(drained[USE[("out",) + s][0]], 1)

            with act.Fori(0, LOOPS) as i:
                for s in range(RING):
                    u = UP0 + s + AHEAD
                    act.wait_ge(raw_in[u % RING], i * 16 + raw_count(u))
                    act.wait_ge(release[u - RING][0], i + release[u - RING][1])
                    act.activation(WHI[:, u % RING, 0:D], RAW[:, u % RING, 0:D], ACT.Copy).then_inc(hi_split, 1)
                    pair, f, _, _ = USE[("up", s)]
                    q, r = s // 2, s % 2
                    act.wait_ge(filled[pair], i + f)
                    act.wait_ge(up_free, i * RING + (s + 1))
                    for a, b, o in pieces(1, 131):
                        last = act.activation(UP[:, q, r, o:o + b - a], PAIR[pair][:, a:b], ACT.Copy)
                    last.then_inc(drained[pair], 1)
                    if r == 1:
                        act.wait_ge(up_free, i * RING + (RING + s + 1))
                        act.activation(CV[:, q, 1, :], CV[:, q, 1, :], ACT.Silu).then_inc(silu_out, 1)
            split[0] += 2 * FT

            act.wait_ge(ff_out, FT + 1)
            for at_, s in enumerate(PLAN_DOWN, UP_STEP + 1):
                split_to(goal[at_])
                if s[0] == "k":
                    chunks_to(chunk_limit(chunk_at[("down",) + s]))
                else:
                    epilogue("down", s[1])

        @block.vector
        def _(dve):
            n_link = [0]

            def link(ins):
                n_link[0] += 1
                ins.then_inc(vlink, 1)
                dve.wait_ge(vlink, n_link[0])

            split = [0]

            def split_to(n):
                while split[0] < n:
                    u = split[0]
                    dve.wait_ge(hi_split, u + 1)
                    wait_slot(dve, u)
                    w = width(u)
                    dve.tensor_tensor(WLO[:, u % RING, 0:w], RAW[:, u % RING, 0:w], WHI[:, u % RING, 0:w].bitcast(F32),
                                      ALU.subtract).then_inc(lo_split, 1)
                    split[0] += 1

            link(dve.memset(SCND[:, :].bitcast(F32), 0.0))
            dve.wait_ge(cond_silu, 1)
            cnd = CND[:, :, :].rearrange("p g c -> p c g")
            parts = SCND[:, 0:4 * KC].rearrange("p (c n) -> p c n", c=KC)
            link(dve.tensor_copy(parts[:, :, 0:4:2], cnd))
            dve.tensor_tensor(parts[:, :, 1:4:2], cnd, parts[:, :, 0:4:2].bitcast(F32), ALU.subtract)\
                .then_inc(cond_split, 1)
            dve.memset(G2[:, :, :, :], 0.0)

            def from_x(g):
                t = wait_filled(dve, ("xt", g))
                dve.tensor_copy(Y[:, :, cols(g)], t[:, :].rearrange("p (c n) -> p c n", c=KC))\
                    .then_inc(drained[USE[("xt", g)][0]], 1)

            for g in range(TILES):
                dve.wait_ge(x_in[g % 2], 16 * (g // 2 + 1))
                if g == 1:
                    dve.wait_ge(pos_in, 16 * 4)
                if g:
                    dve.tensor_tensor(XS[:, g % 2, 0:512], XS[:, g % 2, 0:512], POSR[:, g - 1, :], ALU.add)
                    dve.tensor_tensor(XS[:, g % 2, 512:D], XS[:, g % 2, 512:D], POSC[:, :], ALU.add).then_inc(x_pos, 1)
                    dve.wait_ge(x_pos, g)
                dve.wait_ge(x_root, g + 1)
                link(dve.reciprocal(STAT[:, 0, 2, g:g + 1], STAT[:, 0, 1, g:g + 1]))
                if g >= 2:
                    wait_filled(dve, ("xt", g - 2))
                dve.tensor_scalar(XN[:, g % 2, :], XS[:, g % 2, :], STAT[:, 0, 2, g:g + 1], None, ALU.mult)\
                    .then_inc(x_normed, 1)
                if g == 0:
                    t = wait_filled(dve, "consts")
                    dve.tensor_copy(SCOL[:, :], t[:, 0:44])
                    dve.tensor_copy(BCOL[:, :], t[:, 44:92])
                    dve.tensor_copy(FW[:, :, :], t[:, 92:92 + 3 * 44].rearrange("p (k n) -> p k n", k=3))
                    dve.tensor_copy(WST[:, :, :], t[:, 512:1024].rearrange("p (g n) -> p g n", g=4))\
                        .then_inc(drained[3], 1)
                else:
                    from_x(g - 1)
                split_to(min(g + 1, RING))
            from_x(TILES - 1)
            wait_copied(dve, "consts")
            dve.wait_ge(pool_in, POOL_IN)
            for d in range(2):
                for h in range(HEADS):
                    o, j = DH * (h % 2), h // 2
                    last = dve.tensor_scalar(CST[o:o + DH, d, j, 1, o:o + DH], ONES[o:o + DH, 0:DH],
                                             SCOL[o:o + DH, 40 + 2 * d + j:41 + 2 * d + j], None, ALU.mult)
            last.then_inc(n0_set, 1)

            def modulation(sub):
                for group in range(2):
                    last = dve.scalar_tensor_tensor(out=AMOD[:, sub, group, :],
                                                    in0=MODC[:, 24 * sub + KC:24 * sub + 2 * KC, group], scalar=1.0,
                                                    in1=SCOL[:, 16 * sub:16 * sub + KC], op0=ALU.add, op1=ALU.mult)
                last.then_inc(mod2 if sub else mod1, 1)

            order_p2 = []

            def ada(key, p):
                t = wait_filled(dve, key)
                if order_p2:
                    wait_filled(dve, order_p2[-1])
                dve.tensor_copy(MODROW[:, :], t[0:4, 0:512]).then_inc(drained[USE[key][0]], 1)
                order_p2.append((key[0], "p2", p) if len(key) == 3 else ("p2", p))

            def piece2(key, p):
                t = wait_filled(dve, key)
                if p in (4, 5, 10, 11):
                    n = (4, 5, 10, 11).index(p)
                    dve.wait_ge(bg_in, 32 * (n + 1))
                    c0 = 512 * (p % 2)
                    for group in range(2):
                        last = dve.tensor_tensor(GATE[:, group, c0:c0 + 512], t[:, 512 * group:512 * group + 512],
                                                 BG[:, 1, :], ALU.add)
                    last.then_inc(drained[USE[key][0]], 1)
                    wait_copied(dve, key)
                    for group in range(2):
                        last = dve.tensor_tensor(GATE[:, group, c0:c0 + 512], GATE[:, group, c0:c0 + 512],
                                                 BG[:, 0, :], ALU.mult)
                    last.then_inc(bg_used, 1)
                    dve.wait_ge(bg_used, n + 1)
                else:
                    dve.tensor_tensor(MODC[:, 4 * p:4 * p + 4, :], t[:, 0:8].rearrange("p (m g) -> p m g", g=2),
                                      BCOL[:, 4 * p:4 * p + 4].unsqueeze(2).to_broadcast([P, 4, 2]), ALU.add)\
                        .then_inc(drained[USE[key][0]], 1)
                    if p in (3, 9):
                        wait_copied(dve, key)
                        modulation(int(p == 9))

            def gate_rows():
                dve.wait_ge(softplus, 1)
                link(dve.tensor_tensor(LF[:, :], NM[:, :], LF[:, :], ALU.subtract))
                dve.wait_ge(pool_made, made_all)
                spans = [(r, seg, d) for d, r in ((0, slice(0, 4)), (1, slice(32, 36)))
                         for seg in ((0, CTX), (CTX, TOK))]

                def run(t, r, seg, d):
                    v = t[r, seg[0]:seg[1]]
                    return v[:, ::-1] if d else v

                for r, seg, d in spans:
                    n = seg[1] - seg[0]
                    one = BIG1[r, 0:n]
                    last = dve.tensor_tensor_scan(run(BR, r, seg, d), one, run(LF, r, seg, d), 0.0, ALU.mult, ALU.add)
                link(last)
                wait_copied(dve, ("gi", 0))
                link(dve.tensor_tensor(AR[:, :], AR[:, :], BR[:, :], ALU.subtract))
                for r, seg, d in spans:
                    init = M0[r, :] if seg[0] else 0.0
                    a = run(AR, r, seg, d)
                    last = dve.tensor_tensor_scan(run(NM, r, seg, d), a, a, init, ALU.max, ALU.max)
                link(last)
                link(dve.tensor_scalar(NM[:, :], NM[:, :], -1.0, None, ALU.mult))
                for r, t in ((slice(0, 4), CTX - 1), (slice(32, 36), 0)):
                    dve.tensor_tensor(MS[r, :], BR[r, t:t + 1], NM[r, t:t + 1], ALU.subtract)
                dve.tensor_tensor(WR[:, :, 1, :], NM[:, :].rearrange("p (g n) -> p g n", g=TILES),
                                  BR[:, :].rearrange("p (g n) -> p g n", g=TILES), ALU.subtract)
                for d, r in ((0, slice(0, 4)), (1, slice(32, 36))):
                    for g in range(TILES):
                        if g:
                            first = g == (4 if d else 1)
                            t = P * (g + 1) if d else P * g - 1
                            s1, op = (M0[r, :], ALU.add) if first else (NM[r, t:t + 1], ALU.subtract)
                            dve.tensor_scalar(WR[r, g, 0, :], NM[r, cols(g)], s1, None, op)
                        t = P * g if d else P * g + P - 1
                        last = dve.tensor_scalar(LF[r, cols(g)], AR[r, cols(g)], NM[r, t:t + 1], None, ALU.add)
                last.then_inc(rows_ready, 1)

            def mix(s):
                kind, n = s
                if kind == "ada":
                    ada(s, n)
                elif kind == "p2":
                    piece2(s, n)
                elif kind == "v":
                    t = wait_filled(dve, s)
                    wait_first_reader(dve, s)
                    gb = GB[:, :].rearrange("p (d k h) -> p d k h", d=2, k=2)
                    for b, g in enumerate(range(2 * n, min(2 * n + 2, TILES))):
                        last = dve.tensor_tensor(
                            G2[:, g, :, :].rearrange("p k (d x) -> p d k x", d=2)[:, :, :, 0:HEADS],
                            t[:, 512 * b + DG:512 * b + DG + 16].rearrange("p (d k h) -> p d k h", d=2, k=2),
                            gb, ALU.add)
                    last.then_inc(drained[USE[s][0]], 1)
                elif kind == "gf":
                    t = wait_filled(dve, s)
                    wait_first_reader(dve, s)
                    dve.tensor_scalar(NM[:, :], t[0:64, 0:TOK], 0.0, None, ALU.min).then_inc(drained[USE[s][0]], 1)
                    wait_copied(dve, s)
                    gate_rows()
                elif kind == "mx":
                    t = wait_filled(dve, s)
                    dve.tensor_tensor(SA[:, n, 0:TOK].rearrange("p (g n) -> p g n", g=TILES),
                                      t[:, 0:TOK].rearrange("p (g n) -> p g n", g=TILES),
                                      BSB[:, n:n + 1, :].to_broadcast([P, TILES, P]), ALU.add)\
                        .then_inc(drained[USE[s][0]], 1)
                elif kind == "gu":
                    t = wait_filled(dve, s)
                    wait_copied(dve, ("mx", n))
                    dve.tensor_tensor(Y[:, 2 + n, :].rearrange("p (h n) -> p h n", h=2), halves(t),
                                      SA[:, n, 0:TOK].rearrange("p (h n) -> p h n", h=2), ALU.mult)\
                        .then_inc(drained[USE[s][0]], 1)
                    if n == 1:
                        wait_copied(dve, ("gu", 0))
                        wait_copied(dve, s)
                        dve.memset(SA[:, :, :], 0.0).then_inc(pads_zero, 1)
                elif kind == "ct":
                    t = wait_filled(dve, s)
                    wait_first_reader(dve, s)
                    dve.tensor_copy(COLS[:, :, 0, :],
                                    t[:, 0:TOK].rearrange("p (g k n) -> p g k n", g=TILES, k=2)[:, :, 0, :])\
                        .then_inc(drained[USE[s][0]], 1)
                    wait_copied(dve, s)
                elif kind == "B":
                    g, d = MUNITS[n]
                    dve.wait_ge(psM_full, n + 1)
                    if n:
                        dve.wait_ge(s_ready, n)
                    for h in range(HEADS):
                        last = dve.scalar_tensor_tensor(out=XE[:, h, :], in0=psM[:, cols(h)],
                                                        scalar=COLS[:, g, 0, 32 * d + h:32 * d + h + 1],
                                                        in1=MASK[:, d, :], op0=ALU.add, op1=ALU.min)
                    last.then_inc(xe_ready, 1)
                    dve.wait_ge(we_ready, n + 1)
                    if n:
                        dve.wait_ge(psN_full, n)
                    if g:
                        dve.tensor_tensor(QW[:, :, :], QK[:, 0:2, cols(g)], WE[:, :, 0, :], ALU.mult)\
                            .then_inc(qw_ready, 1)
                    dve.wait_ge(e_ready, n + 1)
                    dve.wait_ge(psQ_full, n + 1)
                    dve.tensor_tensor(SS[:, :, :], XE[:, :, :], psQ.rearrange("p (h n) -> p h n", h=HEADS), ALU.mult)\
                        .then_inc(s_ready, 1)
                elif kind == "C":
                    g, d = MUNITS[n]
                    dve.wait_ge(psN_full, n + 1)
                    num = psN.rearrange("p (j k n) -> p j k n", j=2, k=2)
                    link(dve.scalar_tensor_tensor(out=WE[:, :, 1, :], in0=num[:, :, 1, :], scalar=-1.0,
                                                  in1=WE[:, :, 1, :], op0=ALU.mult, op1=ALU.max))
                    link(dve.tensor_tensor(WE[:, :, 1, :], num[:, :, 1, :], WE[:, :, 1, :], ALU.max))
                    link(dve.reciprocal(WE[:, :, 1, :], WE[:, :, 1, :]))
                    h_out = QW[:, :, :] if d else HA[:, :, cols(g)]
                    dve.tensor_tensor(h_out, num[:, :, 0, :], WE[:, :, 1, :], ALU.mult).then_inc(n_read, 1)
                    if d:
                        dve.wait_ge(n_read, n + 1)
                        link(dve.tensor_tensor(HA[:, :, cols(g)], HA[:, :, cols(g)], QW[:, :, :], ALU.add))
                    if (g, d) in UPD:
                        upd = psM.rearrange("p (j k n) -> p j k n", j=2, k=2)
                        dve.wait_ge(psC_full, UPD.index((g, d)) + 1)
                        t = 0 if d else P - 1
                        for h in range(HEADS):
                            o, j = DH * (h % 2), h // 2
                            r = slice(o, o + DH)
                            if g == 0:
                                dve.tensor_copy(CSO[r, d, j, :], upd[r, j, 0, o:o + DH])
                                last = dve.tensor_copy(NS[r, d, j:j + 1], upd[r, j, 1, 0:1])
                            else:
                                last = dve.scalar_tensor_tensor(out=CST[r, d, j, :, o:o + DH],
                                                                in0=CST[r, d, j, :, o:o + DH],
                                                                scalar=WE[r, j, 0, t:t + 1],
                                                                in1=upd[r, j, :, o:o + DH], op0=ALU.mult, op1=ALU.add)
                        last.then_inc(c_read, 1)
                        dve.wait_ge(c_read, UPD.index((g, d)) + 1)
                elif kind == "cx":
                    t = wait_filled(dve, s)
                    wait_copied(dve, ("cc", n))
                    for a, b, o in pieces(PC_, PS_):
                        last = dve.tensor_tensor(SA[:, 0, o:o + b - a], t[:, a:b], SA[:, 0, o:o + b - a], ALU.mult)
                    last.then_inc(drained[USE[s][0]], 1)
                    wait_copied(dve, s)
                    w = PADW - 2 * PC_
                    if n:
                        wait_copied(dve, ("cb", 0))
                    link(dve.tensor_scalar(SBb[:, 0:w], SA[:, 0, PC_ - 1:PC_ - 1 + w], SCOL[:, 32 + n:33 + n], None,
                                           ALU.mult))
                    link(dve.scalar_tensor_tensor(out=SBb[:, 0:w], in0=SA[:, 0, PC_:PC_ + w],
                                                  scalar=SCOL[:, 34 + n:35 + n], in1=SBb[:, 0:w],
                                                  op0=ALU.mult, op1=ALU.add))
                    dve.scalar_tensor_tensor(out=SBb[:, 0:w], in0=SA[:, 0, PC_ + 1:PC_ + 1 + w],
                                             scalar=SCOL[:, 36 + n:37 + n], in1=SBb[:, 0:w],
                                             op0=ALU.mult, op1=ALU.add).then_inc(conv_done, 1)
                elif kind == "cb":
                    t = wait_filled(dve, s)
                    dve.wait_ge(conv_done, n + 1)
                    y0 = 0
                    for a, b, o in pieces(0, PS_ - PC_):
                        last = dve.tensor_tensor(Y[:, 6 + n, y0:y0 + b - a], t[:, a:b], SBb[:, o:o + b - a], ALU.mult)
                        y0 += b - a
                    last.then_inc(drained[USE[s][0]], 1)
                elif kind == "pz":
                    pool_tile(n)
                elif kind == "o":
                    wait_copied(dve, s)
                    if n == 0:
                        dve.wait_ge(states_out, 16 * 8)
                    dve.tensor_tensor(Y[:, n, :], TMP[:, :], HA[:, n, :], ALU.mult).then_inc(y_made, 1)

            def pool_tile(j):
                wait_copied(dve, ("pz", j))
                z = SA[:, 1, :]
                if j:
                    dve.wait_ge(pooled, 1)
                else:
                    wait_copied(dve, ("cb", 1))
                link(dve.tensor_tensor(SBb[:, 1:PADW], z[:, 0:PADW - 1], z[:, 1:PADW], ALU.add))
                lo, hi = slice(0, 64), slice(64, P)
                a, b = 2, PADW - 1
                if j == 0:
                    link(dve.tensor_tensor(SCb[hi, a:b], SBb[hi, a - 1:b - 1], SBb[hi, a + 1:b + 1], ALU.add))
                else:
                    link(dve.tensor_tensor(SCb[:, a:b], SBb[:, a - 1:b - 1], SBb[:, a + 1:b + 1], ALU.add))
                    a, b = 4, PADW - 4
                    link(dve.tensor_tensor(SBb[:, a:b], SCb[:, a - 2:b - 2], SCb[:, a + 2:b + 2], ALU.add))
                    a, b = 8, PADW - 8
                    link(dve.tensor_tensor(SCb[hi, a:b], SBb[hi, a - 4:b - 4], SBb[hi, a + 4:b + 4], ALU.add))
                for r, t in ((lo, SBb), (hi, SCb)):
                    first, end = EDGE[r, 16 * j:16 * j + 8], EDGE[r, 16 * j + 8:16 * j + 16]
                    for o, w in ((PC_, first), (PS_, first), (PC_ + CTX - 8, end), (PADW - 16, end)):
                        last = dve.tensor_tensor(t[r, o:o + 8], t[r, o:o + 8], w, ALU.mult)
                link(last)
                for r, t in ((lo, SBb), (hi, SCb)):
                    for o, n in ((PC_, CTX), (PS_, TOK - CTX)):
                        last = dve.scalar_tensor_tensor(out=z[r, o:o + n], in0=t[r, o:o + n],
                                                        scalar=EDGE[r, 32 + j:33 + j], in1=z[r, o:o + n],
                                                        op0=ALU.mult, op1=ALU.subtract)
                last.then_inc(pooled, 1)

            for at_, s in enumerate(PLAN):
                if at_ == len(HEAD_STEPS):
                    dve.wait_ge(mod1, 1)
                    for k in range(KC):
                        if k:
                            dve.wait_ge(h_lo, k)
                        for group, a, b in ((0, 0, CTX), (1, CTX, TOK)):
                            last = dve.tensor_scalar(TMP[:, a:b], Y[:, k, a:b], AMOD[:, 0, group, k:k + 1],
                                                     MODC[:, k, group:group + 1], ALU.mult, ALU.add)
                        link(last)
                        dve.wait_ge(h_hi, k + 1)
                        dve.tensor_tensor(Hlo[:, k, :], TMP[:, :], Hhi[:, k, :].bitcast(F32), ALU.subtract)\
                            .then_inc(h_lo, 1)
                split_to(goal[at_])
                mix(s)

            n_chunk_lo = [0]

            def chunks_to(n):
                while n_chunk_lo[0] < n:
                    m = n_chunk_lo[0]
                    src, w = chunk_source(m)
                    dve.wait_ge(act_hi, m + 1)
                    wait_chunk_slot(dve, m)
                    dve.tensor_tensor(ASLO[:, m % 3, 0:w], src, ASHI[:, m % 3, 0:w].bitcast(F32), ALU.subtract)\
                        .then_inc(act_lo, 1)
                    n_chunk_lo[0] += 1

            def epilogue(stage, g):
                n = TILES * (stage == "down") + g
                i = 1 + 2 * (stage == "down")
                key = (stage, "epi", g)
                t = wait_filled(dve, key)
                dve.wait_ge(y_root, n + 1)
                link(dve.reciprocal(STAT[:, i, 2, g:g + 1], STAT[:, i, 1, g:g + 1]))
                if n:
                    dve.wait_ge(x2_new, n)
                dve.scalar_tensor_tensor(out=T2[:, :], in0=t[:, :], scalar=STAT[:, i, 2, g:g + 1],
                                         in1=GATE[:, int(g > 0), :], op0=ALU.mult, op1=ALU.mult)\
                    .then_inc(drained[USE[key][0]], 1)
                wait_copied(dve, key)
                dve.tensor_tensor(X2[:, g, :], T2[:, :], X2[:, g, :], ALU.add).then_inc(x2_new, 1)

            for at_, s in enumerate(PLAN_OUT, len(PLAN)):
                split_to(goal[at_])
                if s[0] == "k":
                    chunks_to(chunk_limit(chunk_at[("out",) + s]))
                    if s == ("k", 0, 3):
                        dve.wait_ge(x2_in, 16 * TILES)
                        dve.wait_ge(pos_in, 16 * 8)
                        for g in range(1, TILES):
                            dve.tensor_tensor(X2[:, g, 0:512], X2[:, g, 0:512], POSR[:, g - 1, :], ALU.add)
                            last = dve.tensor_tensor(X2[:, g, 512:D], X2[:, g, 512:D], POSC[:, :], ALU.add)
                        link(last)
                elif s[0] == "epi":
                    epilogue("out", s[1])
                elif s[0] == "nrm":
                    g = s[1]
                    dve.wait_ge(n_root, g + 1)
                    link(dve.reciprocal(STAT[:, 2, 2, g:g + 1], STAT[:, 2, 1, g:g + 1]))
                    if g:
                        wait_filled(dve, ("out", "tr", g - 1))
                    dve.tensor_scalar(XN2[:, :], X2[:, g, :], STAT[:, 2, 2, g:g + 1], None, ALU.mult)\
                        .then_inc(n_xn, 1)
                elif s[0] == "tr":
                    g = s[1]
                    key = ("out",) + s
                    t = wait_filled(dve, key)
                    wait_first_reader(dve, key)
                    if g:
                        dve.wait_ge(n_lo, g)
                    for k in range(KC):
                        last = dve.tensor_scalar(HT2[:, k, :], t[:, cols(k)], AMOD[:, 1, int(g > 0), k:k + 1],
                                                 MODC[:, 24 + k, int(g > 0):int(g > 0) + 1], ALU.mult, ALU.add)
                    last.then_inc(drained[USE[key][0]], 1)
                    wait_copied(dve, key)
                    dve.tensor_tensor(Hlo[:, :, cols(g)], HT2[:, :, :], Hhi[:, :, cols(g)].bitcast(F32), ALU.subtract)\
                        .then_inc(n_lo, 1)
                elif s[0] == "ada":
                    ada(("out",) + s, s[1])
                elif s[0] == "p2":
                    piece2(("out",) + s, s[1])

            for s in range(RING):
                dve.memset(UP[:, s // 2, s % 2, :], 0.0).then_inc(up_free, 1)
            dve.memset(CV[:, 0, 0, :], 0.0).then_inc(ff_out, 1)
            base, per = n_link[0], 2 * RING
            with dve.Fori(0, LOOPS) as i:
                for s in range(RING):
                    u = UP0 + s + AHEAD
                    dve.wait_ge(hi_split, i * RING + (u + 1))
                    dve.tensor_tensor(WLO[:, u % RING, 0:D], RAW[:, u % RING, 0:D], WHI[:, u % RING, 0:D].bitcast(F32),
                                      ALU.subtract).then_inc(lo_split, 1)
                    pair, _, _, after = USE[("up", s)]
                    q, r = s // 2, s % 2
                    dve.wait_ge(drained[pair], i + after)
                    f = i * 2 + (q + FT * r)
                    if r == 0:
                        dve.wait_ge(ff_out, i * 2 + (q + 1))
                    dve.tensor_scalar(CV[:, q, r, :], UP[:, q, r, 0:AW], FW[:, 0, bass.ds(f, 1)], None, ALU.mult)\
                        .then_inc(vlink, 1)
                    for k in (1, 2):
                        dve.wait_ge(vlink, i * per + (base + 2 * s + k))
                        dve.scalar_tensor_tensor(out=CV[:, q, r, :], in0=UP[:, q, r, k:k + AW],
                                                 scalar=FW[:, k, bass.ds(f, 1)], in1=CV[:, q, r, :],
                                                 op0=ALU.mult, op1=ALU.add).then_inc(vlink if k == 1 else up_free, 1)
                    if r == 1:
                        dve.wait_ge(silu_out, i * 2 + (q + 1))
                        dve.tensor_tensor(ACTF[:, bass.ds(i * 2 + q, 1), :], CV[:, q:q + 1, 0, :], CV[:, q:q + 1, 1, :],
                                          ALU.mult).then_inc(ff_out, 1)
            n_link[0] += LOOPS * per
            split[0] += 2 * FT

            for at_, s in enumerate(PLAN_DOWN, UP_STEP + 1):
                split_to(goal[at_])
                if s[0] == "k":
                    chunks_to(chunk_limit(chunk_at[("down",) + s]))
                else:
                    epilogue("down", s[1])

        @block.tensor
        def _(pe):
            pe.wait_ge(pool_made, 3)
            pe.wait_ge(consts_in, NCONST)
            t = PAIR[3]
            pe.transpose(t[:, 0:44], SMALL[:, :], IDENT[0:44, 0:44])
            pe.transpose(t[:, 44:92], BROWS[:, :], IDENT[0:48, 0:48])
            for k in range(3):
                pe.transpose(t[:, 92 + 44 * k:136 + 44 * k], FROWS[:, k, :], IDENT[0:44, 0:44])
            for w in range(4):
                last = pe.transpose(t[:, 512 + P * w:640 + P * w], WS[:, w, :], IDENT[:, :])
            last.then_inc(filled[3], 1)
            for g in range(TILES):
                pe.wait_ge(x_normed, g + 1)
                t = wait_free(pe, ("xt", g))
                for k in range(KC):
                    last = pe.transpose(t[:, cols(k)], XN[:, g % 2, cols(k)], IDENT[:, :])
                last.then_inc(filled[USE[("xt", g)][0]], 1)

            def ada(key, first):
                t = wait_free(pe, key)
                for q in range(4):
                    u = first + q
                    pe.wait_ge(lo_split, u + 1)
                    for k in range(2):
                        for w in (WHI, WLO):
                            last = pe.matmul(t[:, 0:512], SCND[:, 4 * (2 * q + k):4 * (2 * q + k) + P], w[:, u % RING, 512 * k:512 * k + 512],
                                             start=(q == 0 and k == 0 and w is WHI),
                                             stop=(q == 3 and k == 1 and w is WLO))
                    last.then_inc(ada_used if q < 3 else filled[USE[key][0]], 1)

            def piece2(key, row_key, p):
                wait_copied(pe, row_key)
                t = wait_free(pe, key)
                if p in (4, 5, 10, 11):
                    for group in range(2):
                        last = pe.matmul(t[:, 512 * group:512 * group + 512], SELG[:, group, :], MODROW[:, :],
                                         start=True, stop=True)
                else:
                    for m in range(4):
                        last = pe.matmul(t[:, 2 * m:2 * m + 2], MODROW[:, cols(m)], SELG[:, :, 0],
                                         start=True, stop=True)
                last.then_inc(filled[USE[key][0]], 1)

            def channel_tile(t, n_or_slot, wait_h=False):
                for k in range(KC):
                    if wait_h:
                        pe.wait_ge(h_lo, k + 1)
                    for n, (w, h) in enumerate(((WHI, Hhi), (WHI, Hlo), (WLO, Hhi))):
                        for half in range(2):
                            last = pe.matmul(t[:, 512 * half:512 * half + HALF], w[:, n_or_slot, cols(k)],
                                             h[:, k, HALF * half:HALF * half + HALF],
                                             start=(k == 0 and n == 0), stop=(k == KC - 1 and n == 2))
                return last

            def token_tile(out, g, unit, w):
                for k in range(KC):
                    slot = (unit + k // 4) % RING
                    for n, (wt, h) in enumerate(((WHI, Hhi), (WHI, Hlo), (WLO, Hhi))):
                        last = pe.matmul(out, h[:, k, cols(g)], wt[:, slot, w * (k % 4):w * (k % 4) + w],
                                         start=(k == 0 and n == 0), stop=(k == KC - 1 and n == 2))
                return last

            def mix(s):
                kind, n = s
                if kind == "ada":
                    ada(s, UPTO[s] - 4)
                elif kind == "p2":
                    piece2(s, ("ada", n), n)
                elif kind in FEATURE:
                    u = UPTO[s] - 1
                    t = wait_free(pe, s)
                    pe.wait_ge(lo_split, u + 1)
                    channel_tile(t, u % RING, s == ("q", 0)).then_inc(filled[USE[s][0]], 1)
                elif kind == "v":
                    u = UPTO[s] - 2
                    t = wait_free(pe, s)
                    pe.wait_ge(lo_split, u + 2)
                    for b, g in enumerate(range(2 * n, min(2 * n + 2, TILES))):
                        last = token_tile(t[:, 512 * b:512 * b + DG + 16], g, u, DG + 16)
                    last.then_inc(filled[USE[s][0]], 1)
                elif kind == "gv":
                    u = UPTO[s] - 2
                    t = wait_free(pe, s)
                    pe.wait_ge(lo_split, u + 2)
                    for b, g in enumerate(range(0, 4) if n == 0 else [4]):
                        last = token_tile(t[:, DG * b:DG * b + DG], g, u, DG)
                    last.then_inc(filled[USE[s][0]], 1)
                elif kind in ("gi", "gf"):
                    for v in range(3):
                        wait_copied(pe, ("v", v))
                    t = wait_free(pe, s)
                    for g in range(TILES):
                        last = pe.transpose(t[0:64, cols(g)], G2[:, g, int(kind == "gf"), :], IDENT[:, :])
                    last.then_inc(filled[USE[s][0]], 1)
                elif kind == "kt":
                    for i in range(2):
                        wait_copied(pe, ("k", i))
                    t = wait_free(pe, s)
                    for b, g in enumerate(range(0, 4) if n == 0 else [4]):
                        for j in range(2):
                            last = pe.transpose(t[:, DG * b + P * j:DG * b + P * j + P], QK[:, 2 + j, cols(g)],
                                                IDENT[:, :])
                    last.then_inc(filled[USE[s][0]], 1)
                elif kind == "mx":
                    wait_copied(pe, ("gv", 0))
                    wait_copied(pe, ("gv", 1))
                    t = wait_free(pe, s)
                    for g in range(TILES):
                        for b in range(2):
                            w = 2 * n + b
                            last = pe.matmul(t[DH * b:DH * b + DH, cols(g)], GV[:, g, DH * w:DH * w + DH], WST[:, w, :],
                                             start=True, stop=True)
                    last.then_inc(filled[USE[s][0]], 1)
                elif kind == "ct":
                    pe.wait_ge(rows_ready, 1)
                    t = wait_free(pe, s)
                    for g in range(TILES):
                        for b, src in enumerate((AR, LF)):
                            o = P * g + 64 * b
                            last = pe.transpose(t[:, o:o + 64], src[:, cols(g)], IDENT[0:64, 0:64])
                    last.then_inc(filled[USE[s][0]], 1)
                elif kind == "B":
                    g, d = MUNITS[n]
                    if n == 0:
                        for key in ("xt", 3), ("xt", 4):
                            wait_copied(pe, key)
                        wait_copied(pe, ("ct", 0))
                        for i in range(2):
                            wait_copied(pe, ("q", i))
                    if n:
                        pe.wait_ge(xe_ready, n)
                        pe.wait_ge(c_read, len([u for u in UPD if m_index[u] < n]))
                    for h in range(HEADS):
                        r = 32 * d + h
                        last = pe.matmul(psM[:, cols(h)], IDENT[0:64, r:r + 1].to_broadcast([64, P]), NM[:, cols(g)],
                                         start=True, stop=True)
                    last.then_inc(psM_full, 1)
                    if n:
                        pe.wait_ge(we_ready, n)
                    for j in range(2):
                        last = pe.matmul(psW[:, 2 * P * j:2 * P * j + 2 * P], SELP[:, 2 * d + j, :],
                                         WR[:, g, :, :].rearrange("p k n -> p (k n)"), start=True, stop=True)
                    last.then_inc(psW_full, 1)
                    if n:
                        pe.wait_ge(s_ready, n)
                    for b in range(2):
                        if b:
                            pe.wait_ge(psQ_even, n + 1)
                        r = slice(DH * b, DH * b + DH)
                        for j in range(2):
                            last = pe.matmul(psQ[:, cols(2 * j + b)], QK[r, 2 + j, cols(g)], QK[r, j, cols(g)],
                                             start=True, stop=True)
                        last.then_inc(psQ_full if b else psQ_even, 1)
                elif kind == "C":
                    g, d = MUNITS[n]
                    pe.wait_ge(s_ready, n + 1)
                    carry = g > 0
                    if carry:
                        pe.wait_ge(qw_ready, CARRY.index((g, d)) + 1)
                        pe.wait_ge(n0_set, 1)
                        pe.wait_ge(c_read, len([u for u in UPD if m_index[u] < n]))
                    if n:
                        pe.wait_ge(n_read, n)
                    for j in range(2):
                        for k in range(2):
                            o = P * (2 * j + k)
                            if carry:
                                pe.matmul(psN[:, o:o + P], CST[:, d, j, k, :], QW[:, j, :], start=True, stop=False,
                                          skip_group_check=True)
                            for b in range(2):
                                h = 2 * j + b
                                lhs = ONES[:, 0:DH] if k else V[:, g, DH * h:DH * h + DH]
                                last = pe.matmul(psN[DH * b:DH * b + DH, o:o + P], lhs, SS[:, h, :], start=not carry,
                                                 stop=True, skip_group_check=True)
                    last.then_inc(psN_full, 1)
                    if (g, d) in UPD:
                        pe.wait_ge(kw_ready, UPD.index((g, d)) + 1)
                        for j in range(2):
                            for k in range(2):
                                o = P * (2 * j + k)
                                last = pe.matmul(psM[:, o:o + P], KW[:, cols(j)], ONES[:, :] if k else V[:, g, cols(j)],
                                                 start=True, stop=True)
                        last.then_inc(psC_full, 1)
                elif kind == "pl":
                    pe.wait_ge(pooled, n + 1)
                    t = wait_free(pe, s)
                    for a, b, o in ((0, CTX, PC_), (512, 1024, PS_)):
                        last = pe.matmul(t[:, a:b], PWB[:, n, :], SA[:, 1, o:o + b - a], start=True, stop=True)
                    last.then_inc(filled[USE[s][0]], 1)

            pe.wait_ge(cond_split, 1)
            for s in PLAN:
                mix(s)

            def chunk(stage, s):
                _, half, k = s
                m = chunk_at[(stage,) + s]
                u = chunk_unit[m]
                last_k = (KC if stage == "out" else FT) - 1
                pe.wait_ge(lo_split, u + 1)
                pe.wait_ge(act_lo, m + 1)
                for b, g in enumerate(PASS_TILES[half]):
                    key = (stage, "epi", g)
                    t = PAIR[USE[key][0]]
                    if k == 0:
                        wait_free(pe, key)
                    o = P * b + (2 if stage == "down" and half == 0 and b else 0)
                    for n, (a, w) in enumerate(((ASHI, WHI), (ASLO, WHI), (ASHI, WLO))):
                        for c0 in (0, 512):
                            last = pe.matmul(t[:, c0:c0 + 512], a[:, m % 3, o:o + P], w[:, u % RING, c0:c0 + 512],
                                             start=(k == 0 and n == 0), stop=(k == last_k and n == 2))
                    if k == last_k:
                        last.then_inc(filled[USE[key][0]], 1)
                if k < last_k:
                    last.then_inc(chunk_used, 1)

            pe.wait_ge(n_read, len(MUNITS))
            for s in PLAN_OUT:
                if s[0] == "k":
                    chunk("out", s)
                elif s[0] == "tr":
                    g = s[1]
                    key = ("out",) + s
                    t = wait_free(pe, key)
                    pe.wait_ge(n_xn, g + 1)
                    for k in range(KC):
                        last = pe.transpose(t[:, cols(k)], XN2[:, cols(k)], IDENT[:, :])
                    last.then_inc(filled[USE[key][0]], 1)
                elif s[0] == "ada":
                    ada(("out",) + s, UPTO[("out",) + s] - 4)
                elif s[0] == "p2":
                    piece2(("out",) + s, ("out", "ada", s[1]), s[1])

            pe.wait_ge(n_lo, TILES)
            with pe.Fori(0, LOOPS) as i:
                for s in range(RING):
                    pair, _, before, _ = USE[("up", s)]
                    pe.wait_ge(lo_split, i * RING + (UP0 + s + 1))
                    pe.wait_ge(drained[pair], i + before)
                    channel_tile(PAIR[pair], s).then_inc(filled[pair], 1)
            for s in PLAN_DOWN:
                if s[0] == "k":
                    chunk("down", s)


_INS = ["x_prompt", "x_sample", "state_C", "state_n", "state_m", "c", "c_ctx", "norm_g", "ada_w", "ada_b", "w_in",
        "gate_b", "gmlp_ws", "gmlp_b", "pool_w", "pool_scale", "conv_w", "w_out", "ffn_up", "ffn_conv", "ffn_down"]
_OUTS = [(1, 128, 1024), (1, 512, 1024), (1, 1, 2, 4, 64, 64), (1, 1, 2, 4, 64), (1, 1, 2, 4)]


def _shape_tables():
    import numpy as np
    quarter = D // 4
    omega = (1.0 / (10000.0 ** (np.arange(quarter, dtype=np.float32) / np.float32(quarter)))).astype(np.float32)

    def emb(n):
        a = np.arange(n, dtype=np.float32)[:, None] * omega[None, :]
        return np.concatenate([np.sin(a), np.cos(a)], axis=-1).astype(np.float32)

    grid_w = 64
    rows = emb((TOK - CTX) // grid_w)
    edge = np.ones((P, 34), np.float32)
    for j in range(2):
        for half in range(2):
            w = 2 ** (2 * j + half + 1)
            r = slice(64 * half, 64 * half + 64)
            t = np.arange(8)
            edge[r, 16 * j:16 * j + 8] = w / (np.minimum(t, w // 2) + w // 2)
            back = 8 - t
            edge[r, 16 * j + 8:16 * j + 16] = w / (np.minimum(back, w // 2) + w // 2)
            edge[r, 32 + j] = 1.0 / w
    return {"pos_row": np.ascontiguousarray(rows.reshape(TILES - 1, 2, 512).transpose(1, 0, 2)),
            "pos_col": emb(grid_w), "pool_edge": edge}


def kernel(**inputs):
    import numpy as _np
    import concourse.bacc as _bacc
    from concourse import mybir as _mybir
    from concourse.bass_utils import run_bass_kernel_spmd as _run

    nc = _bacc.Bacc("TRN2", target_bir_lowering=False, num_devices=1)
    tables = _shape_tables()
    arrays, args = {}, []
    for name in _INS + list(tables):
        a = _np.ascontiguousarray(inputs[name] if name in inputs else tables[name])
        arrays[f"in_{name}_dram"] = a
        args.append(nc.dram_tensor(f"in_{name}_dram", a.shape, _mybir.dt.from_np(a.dtype), kind="ExternalInput").ap())
    for i, shape in enumerate(_OUTS):
        args.append(nc.dram_tensor(f"out_{i}_dram", shape, _mybir.dt.float32, kind="ExternalOutput").ap())
    hybrid_trunk_layer(nc, *args)
    r = _run(nc, [arrays], core_ids=[0])
    return tuple(r.results[0][f"out_{i}_dram"] for i in range(len(_OUTS)))
```

```python
from contextlib import ExitStack

import concourse.bass as bass
from concourse import mybir

F32 = mybir.dt.float32
F32R = mybir.dt.float32r
BF16 = mybir.dt.bfloat16
ALU = mybir.AluOpType
ACT = mybir.ActivationFunctionType

P = 128
D = 1024
KC = D // P
TILES = 5
TOK = TILES * P
CTX = P
HALF = TOK // 2
HEADS, DH = 4, 64
DG = 256
D_FF = 2816
FT = D_FF // P
EPS = 1e-6
NEG = -1e30
SLOT = 4 * (DG + 16)
RING = 4
AHEAD = 3

Q0, K0, V0, O0, G0, GU0, GV0, PZ0, CB0, CC0, CX0 = 0, 256, 512, 768, 1024, 1040, 1296, 1552, 1808, 2064, 2320

PADW, PC_, PS_ = 672, 8, 152
UPW = TOK + 4
AW = TOK + 2


HEAD_STEPS = [("xs", 0), ("ad", 0), ("xs", 1), ("consts", 0), ("ad", 1), ("xt", 0), ("rows", 0), ("xs", 2), ("xt", 1),
              ("ad", 2), ("xs", 3), ("xt", 2), ("rows", 1), ("xs", 4), ("ad", 3), ("xt", 3), ("rows", 2), ("xt", 4),
              ("rows", 3)]
MIX_STEPS = [
    ("q", 0), ("q", 1), ("k", 0), ("k", 1), ("v", 0), ("v", 1), ("v", 2), ("kt", 0), ("kt", 1), ("gi", 0), ("gf", 0),
    ("gv", 0), ("gv", 1), ("mx", 0), ("mx", 1), ("gu", 0), ("ct", 0),
    ("B", 0), ("ad", 4), ("C", 0), ("rows", 4), ("gu", 1), ("B", 1), ("ad", 5), ("C", 1), ("rows", 5), ("cc", 0),
    ("B", 2), ("ad", 6), ("C", 2), ("rows", 6), ("cx", 0), ("B", 3), ("ad", 7), ("C", 3), ("rows", 7), ("cb", 0),
    ("B", 4), ("ad", 8), ("C", 4), ("rows", 8), ("cc", 1), ("B", 5), ("ad", 9), ("C", 5), ("rows", 9), ("cx", 1),
    ("B", 6), ("ad", 10), ("C", 6), ("rows", 10), ("cb", 1), ("B", 7), ("ad", 11), ("C", 7), ("rows", 11), ("pz", 0),
    ("ada", 4), ("B", 8), ("p2", 4), ("C", 8), ("pz", 1), ("pl", 0), ("B", 9), ("ada", 5), ("C", 9), ("o", 0),
    ("pl", 1), ("p2", 5), ("o", 1)]
AD_BLOCKS = [range(4 * i, 4 * i + 4) for i in range(4)] + [range(24 + 2 * i, 26 + 2 * i) for i in range(8)]
PLAN = HEAD_STEPS + MIX_STEPS
FEATURE = {"q": Q0, "k": K0, "o": O0, "gu": GU0, "pz": PZ0, "cb": CB0, "cc": CC0, "cx": CX0}
MUNITS = [(0, 0), (0, 1), (1, 0), (2, 0), (3, 0), (4, 0), (4, 1), (3, 1), (2, 1), (1, 1)]
OUT_ORDER = [6, 2, 7, 3, 4, 5, 0, 1]
PASS_TILES = [(0, 1, 2), (3, 4)]
PASS_PAIR = {"out": {0: 0, 1: 1, 2: 2, 3: 3, 4: 0}, "down": {0: 3, 1: 1, 2: 2, 3: 0, 4: 3}}


def k_steps(half, count):
    return [("k", half, n) for n in range(count - 2)] + [("k2", half, count - 2)]


B_OUT, B_DOWN = k_steps(1, KC), k_steps(1, FT)
PLAN_OUT = (k_steps(0, KC) + [("epi", 0)] + B_OUT[0:1] + [("epi", 1), ("nrm", 0)] + B_OUT[1:2] + [("nrm", 1)]
            + B_OUT[2:3] + [("tr", 0), ("epi", 2)] + B_OUT[3:4] + [("hi", 0), ("lo", 0)] + B_OUT[4:5]
            + [("nrm", 2)] + B_OUT[5:6] + [("tr", 1), ("hi", 1)] + B_OUT[6:]
            + [("lo", 1), ("epi", 3), ("epi", 4), ("nrm", 3), ("nrm", 4), ("tr", 2), ("hi", 2), ("ada", 10), ("tr", 3),
               ("hi", 3), ("lo", 2), ("tr", 4), ("hi", 4), ("lo", 3), ("lo", 4), ("p2", 10)])
OUT_PAIR = {("out", "tr", 0): 1, ("out", "tr", 1): 2, ("out", "tr", 2): 1, ("out", "tr", 3): 0, ("out", "tr", 4): 3,
            ("out", "ada", 10): 2, ("out", "p2", 10): 2, ("down", "ada", 11): 0, ("down", "p2", 11): 0}
A_DOWN = k_steps(0, FT)
PLAN_DOWN = ([("ada", 11)] + A_DOWN[0:2] + [("p2", 11)] + A_DOWN[2:] + [("epi", 0)]
             + B_DOWN[0:1] + [("epi", 1)] + B_DOWN[1:2] + [("epi", 2)] + B_DOWN[2:] + [("epi", 3), ("epi", 4)])


def k_chunks(s):
    return [s[2], s[2] + 1] if s[0] == "k2" else [s[2]]


def plan_units():
    units, upto = [], {}
    done_v = done_gv = False
    for s in PLAN:
        if s[0] == "ada":
            units += [("ada", s[1], q) for q in range(4)]
        elif s[0] == "ad":
            units += [("ad", s[1], q) for q in range(len(AD_BLOCKS[s[1]]))]
        elif s[0] in FEATURE:
            units.append(("ft", FEATURE[s[0]] + P * s[1]))
        elif s[0] == "v" and not done_v:
            units += [("vg", 0), ("vg", 1)]
            done_v = True
        elif s[0] == "gv" and not done_gv:
            units += [("gv", 0), ("gv", 1)]
            done_gv = True
        upto[s] = len(units)
    for s in PLAN_OUT:
        if s[0] in ("k", "k2"):
            units += [("out", OUT_ORDER[n]) for n in k_chunks(s)]
        elif s[0] == "ada":
            units += [("ada", s[1], q) for q in range(4)]
        upto[("out",) + s] = len(units)
    up0 = len(units)
    units += [("up", n) for n in range(2 * FT)]
    for s in PLAN_DOWN:
        if s[0] in ("k", "k2"):
            units += [("down", n) for n in k_chunks(s)]
        elif s[0] == "ada":
            units += [("ada", s[1], q) for q in range(4)]
        upto[("down",) + s] = len(units)
    return units, upto, up0


def plan_pairs(loops):
    readers = {"v": 2, "gf": 2, "ct": 2, "tr": 2}
    nfilled, ndrained, out = [0] * 4, [0] * 4, {}

    def use(key, pair, n):
        out[key] = (pair, nfilled[pair] + 1, ndrained[pair], ndrained[pair] + n)
        nfilled[pair] += 1
        ndrained[pair] += n

    turn = 0
    for s in PLAN:
        if s[0] in ("B", "C", "xs"):
            continue
        if s[0] in ("consts", "xt"):
            use(s, 3 if s[0] == "consts" else 2 + s[1] % 2, 1)
            continue
        use(s, turn % 2, readers.get(s[0], 1))
        turn += 1
    for stage, plan in (("out", PLAN_OUT), ("down", PLAN_DOWN)):
        if stage == "down":
            for pair in range(4):
                out[("up", pair)] = (pair, nfilled[pair] + 1, ndrained[pair], ndrained[pair] + 1)
                nfilled[pair] += loops
                ndrained[pair] += loops
        for s in plan:
            if s[0] == "k" and s[2] == 0:
                for g in PASS_TILES[s[1]]:
                    use((stage, "epi", g), PASS_PAIR[stage][g], 1)
            elif s[0] in ("tr", "ada", "p2"):
                use((stage,) + s, OUT_PAIR[(stage,) + s], readers.get(s[0], 1))
    return out


def hybrid_trunk_layer(nc, x_prompt, x_sample, state_C, state_n, state_m, c, c_ctx, norm_g, ada_w, ada_b, w_in,
                       gate_b, gmlp_ws, gmlp_b, pool_w, pool_scale, conv_w, w_out, ffn_up, ffn_conv, ffn_down,
                       pos_row, pos_col, pool_edge, y_prompt, y_sample, new_C, new_n, new_m):
    LOOPS = 2 * FT // RING
    assert LOOPS * RING == 2 * FT
    UNITS, UPTO, UP0 = plan_units()
    assert UP0 % RING == 0
    USE = plan_pairs(LOOPS)
    NU = len(UNITS)
    NCONST, NLATER = 16 * 7, 16 * 6
    POOL_IN = 16 * 14
    POOL_LO = 2
    made_all = 26

    ada_v = ada_w[0].rearrange("(p c) n -> p c n", c=KC)
    win_v = w_in[0].rearrange("(c p) n -> p c n", p=P)
    wout_v = w_out[0].rearrange("(c p) n -> p c n", p=P)
    up_v = ffn_up[0].rearrange("(c p) n -> p c n", p=P)
    down_v = ffn_down[0].rearrange("(c p) n -> p c n", p=P)
    x_tile = [x_prompt[0]] + [x_sample[0, P * i:P * i + P, :] for i in range(TILES - 1)]
    y_tile = [y_prompt[0]] + [y_sample[0, P * i:P * i + P, :] for i in range(TILES - 1)]

    with ExitStack() as ctx:
        sbuf_end = nc.sbuf_usable_end
        place = {"at": (nc.sbuf_base + 31) // 32 * 32}

        def at(name, shape, dt, offset):
            size = 1
            for n in shape[1:]:
                size *= n
            size *= 2 if dt == BF16 else 4
            assert offset + size <= sbuf_end, (name, offset + size - sbuf_end)
            return nc.alloc_sbuf_tensor_at(name, shape, dt, offset=offset), offset + size

        def sb(name, shape, dt=F32):
            t, end = at(name, shape, dt, place["at"])
            place["at"] = (end + 31) // 32 * 32
            return t

        def sem(name):
            return ctx.enter_context(nc.semaphore(name))

        Hhi = sb("Hhi", [P, KC, TOK], F32R)
        Hlo = sb("Hlo", [P, KC, TOK], F32R)
        GATE = sb("GATE", [P, 2, D])
        RAW = sb("RAW", [P, RING, SLOT])
        WHI = sb("WHI", [P, RING, SLOT], F32R)
        WLO = sb("WLO", [P, RING, SLOT], F32R)
        JUNK = sb("JUNK", [P, D], BF16)
        MODROW = sb("MODROW", [4, 512])
        SELHL = sb("SELHL", [4, 2, P])
        IDENT = sb("IDENT", [P, P])
        ONES = sb("ONES", [P, P])
        MODC = sb("MODC", [P, 6 * KC, 2])
        BCOL = sb("BCOL", [P, 6 * KC])
        SCOL = sb("SCOL", [P, 44])
        FW = sb("FW", [P, 3, 2 * FT])
        AMOD = sb("AMOD", [P, 2, 2, KC])
        STAT = sb("STAT", [P, 4, 3, TILES])
        EPSC = sb("EPSC", [P, 1])
        COND = sb("COND", [P, KC, 4])
        CONDHL = sb("CONDHL", [P, 4 * KC + P - 4], F32R)
        bg_at = place["at"]
        BG = sb("BG", [P, 2, 512])
        region = place["at"]

        Y = sb("Y", [P, KC, TOK])
        QK = sb("QK", [P, 4, TOK])
        KT = sb("KT", [P, TILES, DG])
        V = sb("V", [P, TILES, DG])
        GV = sb("GV", [P, TILES, DG])
        WST = sb("WST", [P, 4, P])
        HA = sb("HA", [P, 2, TOK])
        SA = sb("SA", [P, 2, PADW])
        SBb = sb("SBb", [P, PADW])
        SCb = sb("SCb", [P, PADW])
        XE = sb("XE", [P, 4, P])
        SS = sb("SS", [P, 4, P])
        WE = sb("WE", [P, 2, 2, P])
        QW = sb("QW", [P, 2, P])
        KW = sb("KW", [P, DG])
        CST = sb("CST", [P, 2, 2, 2, P])
        LF = sb("LF", [64, TOK])
        BR = sb("BR", [64, TOK])
        AR = sb("AR", [64, TOK])
        NM = sb("NM", [64, TOK])
        WR = sb("WR", [64, TILES, 2, P])
        COLS = sb("COLS", [P, TILES, 2, 64])
        MASK = sb("MASK", [P, 2, P])
        SELP = sb("SELP", [64, 4, P])
        PWB = sb("PWB", [P, 2, P])
        EDGE = sb("EDGE", [P, 34])
        GB = sb("GB", [P, 16])
        M0 = sb("M0", [64, 1])
        MS = sb("MS", [64, 1])
        NS = sb("NS", [P, 2, 2])
        CND = sb("CND", [P, 2, KC])

        base = {}
        cur = region
        for name, size in (("Y", KC * TOK * 4), ("QK", 4 * TOK * 4), ("KT", 5120), ("V", 5120),
                           ("GV", 5120), ("WST", 2048), ("HA", 5120), ("SA", 2 * PADW * 4), ("SBb", PADW * 4),
                           ("SCb", PADW * 4), ("XE", 2048), ("SS", 2048)):
            base[name] = cur
            cur += size
        POSC, _ = at("POSC", [P, 512], F32, base["QK"])
        POSR, _ = at("POSR", [P, 4, 512], F32, base["QK"] + 2048)
        XN, _ = at("XN", [P, 2, D], F32, base["KT"])
        SMALL, _ = at("SMALL", [44, P], F32, base["GV"])
        BROWS, _ = at("BROWS", [48, P], F32, base["GV"] + 512)
        FROWS, _ = at("FROWS", [44, 3, P], F32, base["GV"] + 1024)
        BSB, _ = at("BSB", [P, 2, P], F32, bg_at)
        CSO, _ = at("CSO", [P, 2, 2, DH], F32, base["Y"])
        BIG1, _ = at("BIG1", [36, TOK - CTX], F32, base["SA"] + 3072)
        WS, _ = at("WS", [P, 4, P], F32, base["GV"] + 2560)
        XSA, _ = at("XSA", [P, 2, D], F32, base["HA"])
        XSB, _ = at("XSB", [P, 2, D], F32, base["XE"])
        XS = [XSA[:, 0, :], XSA[:, 1, :], XSB[:, 0, :], XSB[:, 1, :]]
        G2, _ = at("G2", [P, TILES, 2, 64], F32, base["SBb"])
        TMP, _ = at("TMP", [P, TOK], F32, base["SCb"])

        r0 = region
        ACTF, r1 = at("ACTF", [P, FT, AW], F32, r0)
        r1 = (r1 + 31) // 32 * 32
        X2, r2 = at("X2", [P, TILES, D], F32, r1)
        ASHI, r3 = at("ASHI", [P, 3, 392], F32R, r2)
        ASLO, _ = at("ASLO", [P, 3, 392], F32R, r3)
        UP, r4 = at("UP", [P, 2, 2, UPW], F32, r2)
        r4 = (r4 + 31) // 32 * 32
        CV, r5 = at("CV", [P, 2, 2, AW], F32, r4)
        T2, _ = at("T2", [P, D], F32, r4)
        XN2, _ = at("XN2", [P, 2, D], F32, base["KT"])
        HT2, _ = at("HT2", [P, 2, KC, P], F32, base["GV"])

        PAIR = [ctx.enter_context(nc.psum_tensor(f"PAIR{i}", [P, 2 * 512], F32)) for i in range(4)]
        psQ, psM = PAIR[2][:, 0:512], PAIR[2][:, 512:1024]
        psW, psN = PAIR[3][:, 0:512], PAIR[3][:, 512:1024]

        raw_in = [sem(f"raw_in{i}") for i in range(RING)]
        hi_split, lo_split = sem("hi_split"), sem("lo_split")
        ada_used, chunk_used = sem("ada_used"), sem("chunk_used")
        filled = [sem(f"filled{i}") for i in range(4)]
        drained = [sem(f"drained{i}") for i in range(4)]
        consts_in, later_in, pool_in = sem("consts_in"), sem("later_in"), sem("pool_in")
        pos_in, pos_again = sem("pos_in"), sem("pos_again")
        x_in = [sem(f"x_in{i}") for i in range(4)]
        pool_made = sem("pool_made")
        vlink, alink = sem("vlink"), sem("alink")
        cond_in, cond_silu, cond_split = sem("cond_in"), sem("cond_silu"), sem("cond_split")
        n0_set = sem("n0_set")
        x_pos, x_sq, x_root, x_normed = sem("x_pos"), sem("x_sq"), sem("x_root"), sem("x_normed")
        h_act, h_dve = sem("h_act"), sem("h_dve")
        mod1, mod2, h_hi, h_lo = sem("mod1"), sem("mod2"), sem("h_hi"), sem("h_lo")
        softplus, rows_ready = sem("softplus"), sem("rows_ready")
        psQ_even, psQ_full = sem("psQ_even"), sem("psQ_full")
        psM_full, psW_full = sem("psM_full"), sem("psW_full")
        psN_full, psC_full = sem("psN_full"), sem("psC_full")
        xe_ready, e_ready, we_ready = sem("xe_ready"), sem("e_ready"), sem("we_ready")
        s_ready, qw_ready, kw_ready = sem("s_ready"), sem("qw_ready"), sem("kw_ready")
        n_read, c_read, states_out = sem("n_read"), sem("c_read"), sem("states_out")
        pads_zero, conv_done, pooled = sem("pads_zero"), sem("conv_done"), sem("pooled")
        y_made, bg_in, bg_used = sem("y_made"), sem("bg_in"), sem("bg_used")
        x2_in, x2_pos = sem("x2_in"), sem("x2_pos")
        act_hi, act_lo = sem("act_hi"), sem("act_lo")
        y_sq, y_root, x2_new = sem("y_sq"), sem("y_root"), sem("x2_new")
        n_sq, n_root, n_xn = sem("n_sq"), sem("n_root"), sem("n_xn")
        n_hi, n_lo = sem("n_hi"), sem("n_lo")
        up_free, silu_out, ff_out, y_out = sem("up_free"), sem("silu_out"), sem("ff_out"), sem("y_out")

        block = ctx.enter_context(nc.Block())

        m_index = {u: n for n, u in enumerate(MUNITS)}
        UPD = [u for u in MUNITS if u not in ((4, 0), (1, 1))]
        CARRY = [u for u in MUNITS if u[0] > 0]

        def halves(t):
            return t[:, :].rearrange("p (h n) -> p h n", h=2)[:, :, 0:HALF]

        def pieces(o_ctx, o_smp):
            a = HALF - CTX
            return [(0, CTX, o_ctx), (CTX, HALF, o_smp), (512, 512 + HALF, o_smp + a)]

        def cols(g):
            return slice(P * g, P * g + P)

        def wait_filled(eng, key):
            eng.wait_ge(filled[USE[key][0]], USE[key][1])
            return PAIR[USE[key][0]]

        def wait_free(eng, key):
            if USE[key][2]:
                eng.wait_ge(drained[USE[key][0]], USE[key][2])
            return PAIR[USE[key][0]]

        def wait_first_reader(eng, key):
            eng.wait_ge(drained[USE[key][0]], USE[key][2] + 1)

        def wait_copied(eng, key):
            eng.wait_ge(drained[USE[key][0]], USE[key][3])

        def raw_count(n):
            return 16 * sum(2 if UNITS[m][0] == "vg" else 1 for m in range(n % RING, n + 1, RING))

        def width(n):
            return SLOT if UNITS[n][0] == "vg" else D

        def raw_unit(n):
            return UNITS[n][0] == "ada"

        def is_split(n):
            return not raw_unit(n) or 0 <= n - UP0 - 2 * FT < AHEAD

        splits_to = [sum(is_split(m) for m in range(n)) for n in range(NU + 1)]

        def wait_split(eng, n):
            eng.wait_ge(lo_split, splits_to[n + 1])

        def slot_before(n):
            m = n - RING
            while m >= 0 and not is_split(m):
                m -= RING
            return m

        ALL = [("", s) for s in PLAN] + [("out", s) for s in PLAN_OUT] + [("up", None)] + [("down", s) for s in PLAN_DOWN]
        release, goal, n_ada, n_chunk, pos = {}, {}, 0, 0, 0
        for at_, (stage, s) in enumerate(ALL):
            key = s if stage == "" else (stage,) + (s or ())
            if stage == "up":
                for n in range(2 * FT):
                    pair, f, _, _ = USE[("up", n % 4)]
                    release[UP0 + n] = (filled[pair], f + n // 4, at_)
                pos = UP0 + 2 * FT
                goal[at_] = pos
                continue
            end = UPTO[key]
            if s[0] in ("ada", "ad"):
                for q in range(pos, end - 1):
                    n_ada += 1
                    release[q] = (ada_used, n_ada, at_)
                release[end - 1] = (filled[USE[key][0]], USE[key][1], at_)
            elif s[0] == "k" and stage:
                n_chunk += 1
                release[pos] = (chunk_used, n_chunk, at_)
            elif s[0] == "k2":
                u = USE[(stage, "epi", PASS_TILES[s[1]][-1])]
                for q in range(2):
                    release[pos + q] = (filled[u[0]], u[1], at_)
            elif s in (("v", 2), ("gv", 1)):
                for q in (1, 2):
                    release[pos - q] = (filled[USE[key][0]], USE[key][1], at_)
            elif not stage and s[0] in FEATURE:
                release[pos] = (filled[USE[key][0]], USE[key][1], at_)
            pos = end
        for at_, (stage, s) in enumerate(ALL):
            if stage == "up":
                continue
            key = s if stage == "" else (stage,) + s
            n = UPTO[key]
            if stage and s[0] not in ("k", "k2") and key != ("down", "ada", 11):
                goal[at_] = goal[at_ - 1]
                continue
            while n < NU and n < UPTO[key] + AHEAD:
                r = release.get(slot_before(n)) if is_split(n) else None
                if r is not None and (r[2] > at_ or r[2] == at_ and r[0] is not ada_used):
                    break
                n += 1
            goal[at_] = n
        UP_STEP = len(PLAN) + len(PLAN_OUT)
        goal[UP_STEP - 1] = UP0 + AHEAD
        early_hi = {("tr", 3): UP0 + 1, ("tr", 4): UP0 + 2}
        early_lo = {("tr", 4): UP0 + 1, ("lo", 4): UP0 + 2}

        def wait_slot(eng, n):
            m = slot_before(n)
            if m >= 0:
                eng.wait_ge(release[m][0], release[m][1])

        CHUNKS = [(stage, s[1], n) for stage, plan in (("out", PLAN_OUT), ("down", PLAN_DOWN))
                  for s in plan if s[0] in ("k", "k2") for n in k_chunks(s)]
        chunk_at = {c: n for n, c in enumerate(CHUNKS)}
        chunk_unit = [n for n, u in enumerate(UNITS) if u[0] in ("out", "down")]

        def chunk_source(n):
            stage, half, k = CHUNKS[n]
            if stage == "out":
                a, b = ((0, 3 * P), (3 * P, TOK))[half]
                return Y[:, OUT_ORDER[k], a:b], b - a
            a, b = ((0, 3 * P + 2), (3 * P + 2, AW))[half]
            return ACTF[:, k, a:b], b - a

        def chunk_limit(stage, s):
            n = chunk_at[(stage,) + s[1:]]
            return min(n + 3, len(CHUNKS), 2 * KC if CHUNKS[n][0] == "out" else len(CHUNKS))

        def wait_chunk_slot(eng, n):
            if n >= 3:
                r = release[chunk_unit[n - 3]]
                eng.wait_ge(r[0], r[1])

        @block.sync
        def _(sp):
            def source(u):
                if u[0] == "ada":
                    _, p, q = u
                    return [(0, 2, 512, ada_v[:, 2 * q:2 * q + 2, 512 * p:512 * p + 512])]
                if u[0] == "ad":
                    b, n = AD_BLOCKS[u[1]][0], len(AD_BLOCKS[u[1]])
                    return [(0, KC // n, P * n, ada_v[:, KC // n * u[2]:KC // n * (u[2] + 1), P * b:P * (b + n)])]
                if u[0] == "up":
                    f = P * (u[1] // 2) + D_FF * (u[1] % 2)
                    return [(0, KC, P, up_v[:, :, f:f + P])]
                if u[0] == "ft":
                    return [(0, KC, P, win_v[:, :, u[1]:u[1] + P])]
                if u[0] == "vg":
                    q = u[1]
                    return [(0, 4, DG, win_v[:, 4 * q:4 * q + 4, V0:V0 + DG]),
                            (DG, 4, 16, win_v[:, 4 * q:4 * q + 4, G0:G0 + 16])]
                if u[0] == "gv":
                    return [(0, 4, DG, win_v[:, 4 * u[1]:4 * u[1] + 4, GV0:GV0 + DG])]
                return [(0, 1, D, (wout_v if u[0] == "out" else down_v)[:, u[1]:u[1] + 1, :])]

            def wait_raw(n):
                m = n - RING
                if m >= 0 and is_split(m):
                    sp.wait_ge(hi_split, splits_to[m + 1])
                    sp.wait_ge(lo_split, splits_to[m + 1])
                if m >= 0 and raw_unit(m):
                    sp.wait_ge(release[m][0], release[m][1])

            def load(n):
                wait_raw(n)
                slot = RAW[:, n % RING, :]
                for o, a, b, src in source(UNITS[n]):
                    if UNITS[n][0] == "vg":
                        dst = slot.rearrange("p (a b) -> p a b", a=4)[:, :, o:o + b]
                    else:
                        dst = slot[:, 0:a * b].rearrange("p (a b) -> p a b", a=a)
                    sp.dma_start(dst, src).then_inc(raw_in[n % RING], 16)

            consts = [(BROWS[:, :], ada_b[0].rearrange("(b n) -> b n", n=P)),
                      (SMALL[0:32, :], norm_g[0].rearrange("a (b n) -> (a b) n", n=P)),
                      (SMALL[32:38, :], conv_w[0].rearrange("a (b n) -> (a b) n", n=P)),
                      (SMALL[38:40, :], pool_scale[0].rearrange("(b n) -> b n", n=P)),
                      (SMALL[40:44, :], state_n[0, 0].rearrange("d (j h) e -> (d j) (h e)", h=2)),
                      (FROWS[:, :, :], ffn_conv[0].rearrange("k (b n) -> b k n", n=P)),
                      (WS[:, :, :], gmlp_ws[0].rearrange("g t s -> t g s"))]
            later = [(EDGE[:, :], pool_edge), (GB[:, :], gate_b[0].rearrange("a h -> (a h)").partition_broadcast(P))]
            for w in range(4):
                later.append((BSB[DH * (w % 2):DH * (w % 2) + DH, w // 2, :], gmlp_b[0, w].partition_broadcast(DH)))
            assert NCONST == 16 * len(consts) and NLATER == 16 * len(later)
            for n in range(UP0):
                load(n)
                if n == 3:
                    for h in range(2):
                        sp.dma_start(POSC[64 * h:64 * h + 64, :], pos_col).then_inc(pos_in, 16)
                        sp.dma_start(POSR[64 * h:64 * h + 64, :, :], pos_row[h].partition_broadcast(64)).then_inc(pos_in, 16)
                    for g in (2, 3):
                        sp.dma_start(XS[g], x_tile[g]).then_inc(x_in[g], 16)
                elif RING <= n < RING + 2:
                    for dst, src in consts[4 * (n - RING):4 * (n - RING) + 4]:
                        sp.dma_start(dst, src).then_inc(consts_in, 16)
                elif 2 * KC <= n < 2 * KC + len(later):
                    dst, src = later[n - 2 * KC]
                    sp.dma_start(dst, src).then_inc(later_in, 16)
            for s in range(RING):
                load(UP0 + s)
            with sp.Fori(1, LOOPS) as i:
                for s in range(RING):
                    sp.wait_ge(hi_split, i * RING + (splits_to[UP0] + s - RING + 1))
                    sp.wait_ge(lo_split, i * RING + (splits_to[UP0] + s - RING + 1))
                    col = i * (2 * P) + ((s // 2) * P + (s % 2) * D_FF)
                    sp.dma_start(RAW[:, s, 0:D].rearrange("p (a b) -> p a b", a=KC),
                                 up_v[:, :, bass.ds(col, P)]).then_inc(raw_in[s], 16)
            for n in range(UP0 + 2 * FT, NU):
                load(n)
            for g in range(TILES):
                sp.wait_ge(x2_new, TILES + g + 1)
                sp.dma_start(y_tile[g], X2[:, g, :]).then_inc(y_out, 16)
            sp.wait_ge(y_out, 16 * TILES)
            sp.wait_ge(states_out, 16 * 8)

        @block.gpsimd
        def _(pool):
            made = [0]

            def make(ins):
                made[0] += 1
                ins.then_inc(pool_made, 1)
                pool.wait_ge(pool_made, made[0])

            make(pool.memset(COND[:, :, :], 0.0))
            make(pool.memset(IDENT[:, :], 0.0))
            make(pool.affine_select(out=IDENT[:, :], in_=IDENT[:, :], compare_op=ALU.not_equal, fill=1.0, base=0,
                                    pattern=[[-1, P]], channel_multiplier=1))
            make(pool.memset(ONES[:, :], 1.0))
            make(pool.memset(EPSC[:, :], EPS))
            make(pool.memset(SELHL[:, :, :], 1.0))
            make(pool.affine_select(out=SELHL[:, :, :], in_=SELHL[:, :, :], compare_op=ALU.is_ge, fill=0.0, base=0,
                                    pattern=[[-2, 2], [0, P]], channel_multiplier=1))
            make(pool.affine_select(out=SELHL[:, :, :], in_=SELHL[:, :, :], compare_op=ALU.is_ge, fill=0.0, base=1,
                                    pattern=[[2, 2], [0, P]], channel_multiplier=-1))
            for g in range(1, TILES):
                pool.wait_ge(x_in[g % 4], 16 * (g // 4 + 1))
                if g == 1:
                    pool.wait_ge(pos_in, 16 * 4)
                x = XS[g % 4]
                pool.tensor_tensor(x[:, 0:512], x[:, 0:512], POSR[:, g - 1, :], ALU.add)
                pool.tensor_tensor(x[:, 512:D], x[:, 512:D], POSC[:, :], ALU.add).then_inc(x_pos, 1)
            make(pool.memset(MASK[:, :, :], 0.0))
            make(pool.affine_select(out=MASK[:, 0, :], in_=MASK[:, 0, :], compare_op=ALU.is_ge, fill=NEG, base=0,
                                    pattern=[[1, P]], channel_multiplier=-1))
            make(pool.affine_select(out=MASK[:, 1, :], in_=MASK[:, 1, :], compare_op=ALU.is_ge, fill=NEG, base=0,
                                    pattern=[[-1, P]], channel_multiplier=1))
            for d in range(2):
                for h in range(HEADS):
                    o = DH * (h % 2)
                    r = 32 * d + h
                    make(pool.tensor_copy(SELP[:, 2 * d + h // 2, o:o + DH], IDENT[0:64, r:r + 1].to_broadcast([64, DH])))
            make(pool.memset(M0[:, :], 0.0))
            make(pool.memset(BR[:, :], 0.0))
            make(pool.memset(WR[:, :, :, :], 0.0))
            make(pool.memset(MS[:, :], 0.0))
            make(pool.memset(CST[:, :, :, :, :], 0.0))
            make(pool.memset(PWB[:, :, :], 0.0))
            make(pool.memset(BIG1[:, :], 1.0))
            assert made[0] == made_all
            for d in range(2):
                pool.dma_start(M0[32 * d:32 * d + 4, :], state_m[0, 0, d].unsqueeze(1)).then_inc(pool_in, 16)
                for h in range(HEADS):
                    o = DH * (h % 2)
                    pool.dma_start(CST[o:o + DH, d, h // 2, 0, o:o + DH], state_C[0, 0, d, h]).then_inc(pool_in, 16)
            for w in range(4):
                o = DH * (w % 2)
                pool.dma_start(PWB[o:o + DH, w // 2, o:o + DH], pool_w[0, w]).then_inc(pool_in, 16)

            def gate_rows(n, p):
                if n:
                    pool.wait_ge(bg_used, n)
                col = 512 * (p % 2)
                pool.dma_start(BG[:, 0, :], norm_g[0, 1 if p < 6 else 3, col:col + 512].partition_broadcast(P))\
                    .then_inc(bg_in, 16)
                pool.dma_start(BG[:, 1, :], ada_b[0, 512 * p:512 * p + 512].partition_broadcast(P)).then_inc(bg_in, 16)

            wait_copied(pool, ("mx", 1))
            gate_rows(0, 4)
            wait_copied(pool, ("ct", 0))
            wait_copied(pool, ("kt", 0))
            wait_copied(pool, ("kt", 1))
            for n, (g, d) in enumerate(UPD):
                if n:
                    pool.wait_ge(psC_full, n)
                w = COLS[:, g, 1, 32 * d:32 * d + HEADS].unsqueeze(2).to_broadcast([P, HEADS, DH])
                pool.tensor_tensor(KW[:, :].rearrange("p (h e) -> p h e", h=HEADS),
                                   KT[:, g, :].rearrange("p (h e) -> p h e", h=HEADS), w, ALU.mult)\
                    .then_inc(kw_ready, 1)
            gate_rows(1, 5)
            pool.wait_ge(y_made, 2)
            for g in range(TILES):
                pool.dma_start(X2[:, g, :], x_tile[g]).then_inc(x2_in, 16)
            for n in range(2):
                pool.dma_start(POSC[64 * n:64 * n + 64, :], pos_col).then_inc(pos_again, 16)
                pool.dma_start(POSR[64 * n:64 * n + 64, :, :], pos_row[n].partition_broadcast(64)).then_inc(pos_again, 16)
            pool.wait_ge(x2_in, 16 * TILES)
            pool.wait_ge(pos_again, 16 * 4)
            for g in range(1, TILES):
                pool.tensor_tensor(X2[:, g, 0:512], X2[:, g, 0:512], POSR[:, g - 1, :], ALU.add)
                pool.tensor_tensor(X2[:, g, 512:D], X2[:, g, 512:D], POSC[:, :], ALU.add).then_inc(x2_pos, 1)
            gate_rows(2, 10)
            for g in range(POOL_LO):
                wait_copied(pool, ("out", "tr", g))
                pool.wait_ge(n_hi, g + 1)
                pool.tensor_tensor(Hlo[:, :, cols(g)], HT2[:, g % 2, :, :], Hhi[:, :, cols(g)].bitcast(F32), ALU.subtract)\
                    .then_inc(n_lo, 1)
            wait_filled(pool, ("out", "epi", TILES - 1))
            for s in range(RING):
                pool.memset(UP[:, s // 2, s % 2, :], 0.0).then_inc(up_free, 1)
            pool.wait_ge(x2_new, TILES)
            pool.memset(CV[:, 0, 0, :], 0.0).then_inc(ff_out, 1)
            gate_rows(3, 11)

        @block.scalar
        def _(act):
            n_link = [0]

            def link(ins):
                n_link[0] += 1
                ins.then_inc(alink, 1)
                act.wait_ge(alink, n_link[0])

            act.dma_start(CND[:, 0, :], c_ctx.rearrange("(p c) -> p c", c=KC)).then_inc(cond_in, 16)
            act.dma_start(CND[:, 1, :], c[0].rearrange("(p c) -> p c", c=KC)).then_inc(cond_in, 16)
            for g in range(2):
                act.dma_start(XS[g], x_tile[g]).then_inc(x_in[g], 16)
            act.wait_ge(cond_in, 32)
            act.wait_ge(pool_made, 1)
            act.activation(COND[:, :, 0:4:2], CND[:, :, :].rearrange("p g c -> p c g"), ACT.Silu).then_inc(cond_silu, 1)

            split = [0]

            def split_to(n):
                while split[0] < n:
                    u = split[0]
                    split[0] += 1
                    if not is_split(u):
                        continue
                    act.wait_ge(raw_in[u % RING], raw_count(u))
                    wait_slot(act, u)
                    act.activation(WHI[:, u % RING, 0:width(u)], RAW[:, u % RING, 0:width(u)], ACT.Copy)\
                        .then_inc(hi_split, 1)

            def scaled_copy(dst, src, sub, group, k):
                return act.activation(dst, src, ACT.Identity, scale=AMOD[:, sub, group, k:k + 1],
                                      bias=MODC[:, (24 * sub) + k, group:group + 1])

            def modulate(k):
                scaled_copy(Y[:, k, 0:CTX], Y[:, k, 0:CTX], 0, 0, k)
                scaled_copy(Y[:, k, CTX:TOK], Y[:, k, CTX:TOK], 0, 1, k).then_inc(h_act, 1)

            def mix(s):
                kind, n = s
                if kind == "xs":
                    if n == 0:
                        act.wait_ge(x_in[0], 16)
                        act.wait_ge(pool_made, 5)
                    else:
                        act.wait_ge(x_pos, n)
                    act.activation(JUNK[:, :], XS[n % 4], ACT.Square, accum_out=STAT[:, 0, 0, n:n + 1])\
                        .then_inc(x_sq, 1)
                    act.wait_ge(x_sq, n + 1)
                    act.activation(STAT[:, 0, 1, n:n + 1], STAT[:, 0, 0, n:n + 1], ACT.Sqrt, bias=EPSC[:, :],
                                   scale=1.0 / D).then_inc(x_root, 1)
                    if n == 1:
                        act.wait_ge(x_normed, 1)
                        act.dma_start(XS[0], x_tile[4]).then_inc(x_in[0], 16)
                elif kind == "xt":
                    t = wait_filled(act, s)
                    act.activation(Y[:, :, cols(n)], t[:, :].rearrange("p (c n) -> p c n", c=KC), ACT.Copy)\
                        .then_inc(drained[USE[s][0]], 1)
                elif kind in ("q", "k"):
                    t = wait_filled(act, s)
                    i = 2 * (kind == "k") + n
                    if i == 0:
                        act.wait_ge(x_normed, TILES)
                    act.activation(QK[:, i, :].rearrange("p (h n) -> p h n", h=2), halves(t), ACT.Copy,
                                   scale=DH ** -0.5 if kind == "k" else 1.0).then_inc(drained[USE[s][0]], 1)
                elif kind == "v":
                    t = wait_filled(act, s)
                    g0, g1 = 2 * n, min(2 * n + 2, TILES)
                    act.activation(V[:, g0:g1, :], t[:, :].rearrange("p (g n) -> p g n", g=2)[:, 0:g1 - g0, 0:DG],
                                   ACT.Copy).then_inc(drained[USE[s][0]], 1)
                elif kind == "gi":
                    t = wait_filled(act, s)
                    act.activation(AR[:, :], t[0:64, 0:TOK], ACT.Copy).then_inc(drained[USE[s][0]], 1)
                elif kind == "gf":
                    t = wait_filled(act, s)
                    act.activation(LF[:, :], t[0:64, 0:TOK], ACT.Abs).then_inc(drained[USE[s][0]], 1)
                    wait_first_reader(act, s)
                    link(act.activation(LF[:, :], LF[:, :], ACT.Exp, scale=-1.0))
                    act.activation(LF[:, :], LF[:, :], ACT.Ln, bias=ONES[0:64, 0:1]).then_inc(softplus, 1)
                elif kind in ("kt", "gv"):
                    t = wait_filled(act, s)
                    g0, g1 = (0, 4) if n == 0 else (4, 5)
                    act.activation((KT if kind == "kt" else GV)[:, g0:g1, :],
                                   t[:, 0:DG * (g1 - g0)].rearrange("p (g n) -> p g n", n=DG),
                                   ACT.Copy).then_inc(drained[USE[s][0]], 1)
                elif kind == "ct":
                    t = wait_filled(act, s)
                    act.activation(COLS[:, :, 1, :], t[:, 0:TOK].rearrange("p (g k n) -> p g k n", g=TILES, k=2)[:, :, 1, :],
                                   ACT.Exp).then_inc(drained[USE[s][0]], 1)
                elif kind == "B":
                    g, d = MUNITS[n]
                    act.wait_ge(psW_full, n + 1)
                    if n:
                        act.wait_ge(n_read, n)
                        act.wait_ge(c_read, len([u for u in UPD if m_index[u] < n]))
                    act.activation(WE[:, :, :, :], psW.rearrange("p (j k n) -> p j k n", j=2, k=2), ACT.Exp)\
                        .then_inc(we_ready, 1)
                    act.wait_ge(xe_ready, n + 1)
                    act.activation(XE[:, :, :], XE[:, :, :], ACT.Exp).then_inc(e_ready, 1)
                elif kind == "C" and n == 2:
                    act.wait_ge(c_read, 2)
                    for d in range(2):
                        act.dma_start(new_C[0, 0, d].rearrange("(j h) d e -> (h d) j e", h=2), CSO[:, d, :, :])\
                            .then_inc(states_out, 16)
                        for j in range(2):
                            act.dma_start(new_n[0, 0, d, 2 * j:2 * j + 2, :].rearrange("h e -> (h e)").unsqueeze(1),
                                          NS[:, d, j:j + 1]).then_inc(states_out, 16)
                        act.dma_start(new_m[0, 0, d].unsqueeze(1), MS[32 * d:32 * d + 4, :]).then_inc(states_out, 16)
                elif kind in ("cc", "pz"):
                    t = wait_filled(act, s)
                    act.wait_ge(pads_zero, 1)
                    if n:
                        if kind == "cc":
                            act.wait_ge(conv_done, 1)
                        else:
                            wait_filled(act, ("pl", 0))
                    for a, b, o in pieces(PC_, PS_):
                        last = act.activation(SA[:, int(kind == "pz"), o:o + b - a], t[:, a:b], ACT.Copy)
                    last.then_inc(drained[USE[s][0]], 1)
                elif kind == "pl":
                    t = wait_filled(act, s)
                    for a, b, o in ((0, CTX, 0), (512, 1024, CTX)):
                        last = act.activation(Y[:, 4 + n, o:o + b - a], t[:, a:b], ACT.Copy,
                                              scale=SCOL[:, 38 + n:39 + n])
                    last.then_inc(drained[USE[s][0]], 1)
                elif kind == "o":
                    t = wait_filled(act, s)
                    if n:
                        act.wait_ge(y_made, 1)
                    act.activation(TMP[:, :].rearrange("p (h n) -> p h n", h=2), halves(t), ACT.Sigmoid)\
                        .then_inc(drained[USE[s][0]], 1)

            n_chunk_hi = [0]

            def chunks_to(n):
                while n_chunk_hi[0] < n:
                    m = n_chunk_hi[0]
                    src, w = chunk_source(m)
                    stage, half, k = CHUNKS[m]
                    if stage == "out" and half == 0:
                        y = OUT_ORDER[k]
                        if y < 2:
                            act.wait_ge(y_made, y + 1)
                        else:
                            wait_copied(act, ({1: "gu", 2: "pl", 3: "cb"}[y // 2], y % 2))
                    wait_chunk_slot(act, m)
                    act.activation(ASHI[:, m % 3, 0:w], src, ACT.Copy).then_inc(act_hi, 1)
                    n_chunk_hi[0] += 1

            for at_, s in enumerate(PLAN):
                if at_ == len(HEAD_STEPS):
                    act.wait_ge(mod1, 1)
                    for g in range(TILES - 2, TILES):
                        wait_copied(act, ("xt", g))
                    modulate(0)
                    for k in range(KC):
                        if k % 2:
                            act.wait_ge(h_dve, k // 2 + 1)
                        else:
                            act.wait_ge(h_act, k // 2 + 1)
                        act.activation(Hhi[:, k, :], Y[:, k, :], ACT.Copy).then_inc(h_hi, 1)
                        if k % 2 == 0 and k + 2 < KC:
                            modulate(k + 2)
                split_to(goal[at_])
                if s == ("o", 1):
                    chunks_to(3)
                mix(s)

            def epilogue(stage, g):
                n = TILES * (stage == "down") + g
                t = wait_filled(act, (stage, "epi", g))
                i = 1 + 2 * (stage == "down")
                act.activation(JUNK[:, :], t[:, :], ACT.Square, accum_out=STAT[:, i, 0, g:g + 1]).then_inc(y_sq, 1)
                act.wait_ge(y_sq, n + 1)
                act.activation(STAT[:, i, 1, g:g + 1], STAT[:, i, 0, g:g + 1], ACT.Sqrt, bias=EPSC[:, :],
                               scale=1.0 / D).then_inc(y_root, 1)

            for at_, s in enumerate(PLAN_OUT, len(PLAN)):
                if s[0] in ("k", "k2"):
                    chunks_to(chunk_limit("out", s))
                split_to(early_hi.get(s, goal[at_]))
                if s[0] == "epi":
                    epilogue("out", s[1])
                elif s[0] == "nrm":
                    g = s[1]
                    act.wait_ge(x2_new, g + 1)
                    act.activation(JUNK[:, :], X2[:, g, :], ACT.Square, accum_out=STAT[:, 2, 0, g:g + 1])\
                        .then_inc(n_sq, 1)
                    act.wait_ge(n_sq, g + 1)
                    act.activation(STAT[:, 2, 1, g:g + 1], STAT[:, 2, 0, g:g + 1], ACT.Sqrt, bias=EPSC[:, :],
                                   scale=1.0 / D).then_inc(n_root, 1)
                elif s[0] == "tr":
                    g = s[1]
                    t = wait_filled(act, ("out",) + s)
                    if g == 0:
                        act.wait_ge(mod2, 1)
                    elif g > 1:
                        act.wait_ge(n_lo, g - 1)
                    for k in range(KC // 2):
                        last = scaled_copy(HT2[:, g % 2, k, :], t[:, cols(k)], 1, int(g > 0), k)
                    last.then_inc(drained[USE[("out",) + s][0]], 1)
                elif s[0] == "hi":
                    g = s[1]
                    wait_copied(act, ("out", "tr", g))
                    act.activation(Hhi[:, :, cols(g)], HT2[:, g % 2, :, :], ACT.Copy).then_inc(n_hi, 1)

            with act.Fori(0, LOOPS) as i:
                for s in range(RING):
                    u = UP0 + s + AHEAD
                    act.wait_ge(raw_in[u % RING], i * 16 + raw_count(u))
                    before, f, _, _ = USE[("up", (s - 1) % RING)]
                    act.wait_ge(filled[before], i + (f if s else f - 1))
                    act.activation(WHI[:, u % RING, 0:D], RAW[:, u % RING, 0:D], ACT.Copy).then_inc(hi_split, 1)
                    pair, f, _, _ = USE[("up", s)]
                    q, r = s // 2, s % 2
                    act.wait_ge(filled[pair], i + f)
                    act.wait_ge(up_free, i * RING + (s + 1))
                    for a, b, o in pieces(1, 131):
                        last = act.activation(UP[:, q, r, o:o + b - a], PAIR[pair][:, a:b], ACT.Copy)
                    last.then_inc(drained[pair], 1)
                    if r == 1:
                        act.wait_ge(up_free, i * RING + (RING + s + 1))
                        act.activation(CV[:, q, 1, :], CV[:, q, 1, :], ACT.Silu).then_inc(silu_out, 1)
            split[0] += 2 * FT

            split_to(UP0 + 2 * FT + 5)
            act.wait_ge(ff_out, FT + 1)
            for at_, s in enumerate(PLAN_DOWN, UP_STEP + 1):
                if s == ("ada", 11):
                    chunks_to(2 * KC + 3)
                elif s[0] in ("k", "k2"):
                    chunks_to(chunk_limit("down", s))
                split_to(goal[at_])
                if s[0] == "epi":
                    epilogue("down", s[1])

        @block.vector
        def _(dve):
            n_link = [0]

            def link(ins):
                n_link[0] += 1
                ins.then_inc(vlink, 1)
                dve.wait_ge(vlink, n_link[0])

            split = [0]

            def split_to(n):
                while split[0] < n:
                    u = split[0]
                    split[0] += 1
                    if not is_split(u):
                        continue
                    dve.wait_ge(hi_split, splits_to[u + 1])
                    wait_slot(dve, u)
                    w = width(u)
                    dve.tensor_tensor(WLO[:, u % RING, 0:w], RAW[:, u % RING, 0:w], WHI[:, u % RING, 0:w].bitcast(F32),
                                      ALU.subtract).then_inc(lo_split, 1)

            link(dve.memset(CONDHL[:, :].bitcast(F32), 0.0))
            dve.wait_ge(cond_silu, 1)
            parts = CONDHL[:, 0:4 * KC].rearrange("p (c n) -> p c n", c=KC)
            link(dve.tensor_copy(parts[:, :, 0:4:2], COND[:, :, 0:4:2]))
            dve.tensor_tensor(parts[:, :, 1:4:2], COND[:, :, 0:4:2], parts[:, :, 0:4:2].bitcast(F32), ALU.subtract)\
                .then_inc(cond_split, 1)
            dve.memset(G2[:, :, :, :], 0.0)

            def modulation(sub):
                for group in range(2):
                    last = dve.scalar_tensor_tensor(out=AMOD[:, sub, group, :],
                                                    in0=MODC[:, 24 * sub + KC:24 * sub + 2 * KC, group], scalar=1.0,
                                                    in1=SCOL[:, 16 * sub:16 * sub + KC], op0=ALU.add, op1=ALU.mult)
                last.then_inc(mod2 if sub else mod1, 1)

            def shift_scale(s):
                t = wait_filled(dve, s)
                b, n = AD_BLOCKS[s[1]][0], len(AD_BLOCKS[s[1]])
                dve.tensor_tensor(MODC[:, b:b + n, :], t[:, 0:2 * n].rearrange("p (m g) -> p m g", g=2),
                                  BCOL[:, b:b + n].unsqueeze(2).to_broadcast([P, n, 2]), ALU.add)\
                    .then_inc(drained[USE[s][0]], 1)
                if b + n in (2 * KC, 5 * KC):
                    wait_copied(dve, s)
                    modulation(int(b > 2 * KC))

            order_p2 = []

            def take_rows(key, width, reader):
                t = wait_filled(dve, key)
                if order_p2:
                    wait_filled(dve, order_p2[-1])
                dve.tensor_copy(MODROW[:, 0:width], t[0:4, 0:width]).then_inc(drained[USE[key][0]], 1)
                order_p2.append(reader)

            def ada(key, p):
                take_rows(key, 512, key[:-2] + ("p2", p))

            def piece2(key, p):
                t = wait_filled(dve, key)
                n = (4, 5, 10, 11).index(p)
                dve.wait_ge(bg_in, 32 * (n + 1))
                c0 = 512 * (p % 2)
                for group in range(2):
                    last = dve.tensor_tensor(GATE[:, group, c0:c0 + 512], t[:, 512 * group:512 * group + 512],
                                             BG[:, 1, :], ALU.add)
                last.then_inc(drained[USE[key][0]], 1)
                wait_copied(dve, key)
                for group in range(2):
                    last = dve.tensor_tensor(GATE[:, group, c0:c0 + 512], GATE[:, group, c0:c0 + 512],
                                             BG[:, 0, :], ALU.mult)
                last.then_inc(bg_used, 1)
                dve.wait_ge(bg_used, n + 1)

            def gate_rows():
                dve.wait_ge(softplus, 1)
                link(dve.tensor_tensor(LF[:, :], NM[:, :], LF[:, :], ALU.subtract))
                dve.wait_ge(pool_made, made_all)
                spans = [(r, seg, d) for d, r in ((0, slice(0, 4)), (1, slice(32, 36)))
                         for seg in ((0, CTX), (CTX, TOK))]

                def run(t, r, seg, d):
                    v = t[r, seg[0]:seg[1]]
                    return v[:, ::-1] if d else v

                for r, seg, d in spans:
                    n = seg[1] - seg[0]
                    one = BIG1[r, 0:n]
                    last = dve.tensor_tensor_scan(run(BR, r, seg, d), one, run(LF, r, seg, d), 0.0, ALU.mult, ALU.add)
                link(last)
                wait_copied(dve, ("gi", 0))
                link(dve.tensor_tensor(AR[:, :], AR[:, :], BR[:, :], ALU.subtract))
                for r, seg, d in spans:
                    init = M0[r, :] if seg[0] else 0.0
                    a = run(AR, r, seg, d)
                    last = dve.tensor_tensor_scan(run(NM, r, seg, d), a, a, init, ALU.max, ALU.max)
                link(last)
                link(dve.tensor_scalar(NM[:, :], NM[:, :], -1.0, None, ALU.mult))
                for r, t in ((slice(0, 4), CTX - 1), (slice(32, 36), 0)):
                    dve.tensor_tensor(MS[r, :], BR[r, t:t + 1], NM[r, t:t + 1], ALU.subtract)
                dve.tensor_tensor(WR[:, :, 1, :], NM[:, :].rearrange("p (g n) -> p g n", g=TILES),
                                  BR[:, :].rearrange("p (g n) -> p g n", g=TILES), ALU.subtract)
                for d, r in ((0, slice(0, 4)), (1, slice(32, 36))):
                    for g in range(TILES):
                        if g:
                            first = g == (4 if d else 1)
                            t = P * (g + 1) if d else P * g - 1
                            s1, op = (M0[r, :], ALU.add) if first else (NM[r, t:t + 1], ALU.subtract)
                            dve.tensor_scalar(WR[r, g, 0, :], NM[r, cols(g)], s1, None, op)
                        t = P * g if d else P * g + P - 1
                        last = dve.tensor_scalar(LF[r, cols(g)], AR[r, cols(g)], NM[r, t:t + 1], None, ALU.add)
                last.then_inc(rows_ready, 1)

            def mix(s):
                kind, n = s
                if kind == "ada":
                    ada(s, n)
                elif kind == "ad":
                    take_rows(s, P * len(AD_BLOCKS[n]), ("rows", n))
                elif kind == "rows":
                    shift_scale(s)
                elif kind == "p2":
                    piece2(s, n)
                elif kind == "xs":
                    if n == 0:
                        dve.wait_ge(x_in[0], 16)
                    else:
                        dve.wait_ge(x_pos, n)
                    dve.wait_ge(x_root, n + 1)
                    link(dve.reciprocal(STAT[:, 0, 2, n:n + 1], STAT[:, 0, 1, n:n + 1]))
                    if n >= 2:
                        wait_filled(dve, ("xt", n - 2))
                    dve.tensor_scalar(XN[:, n % 2, :], XS[n % 4], STAT[:, 0, 2, n:n + 1], None, ALU.mult)\
                        .then_inc(x_normed, 1)
                elif kind == "consts":
                    t = wait_filled(dve, s)
                    dve.tensor_copy(SCOL[:, :], t[:, 0:44])
                    dve.tensor_copy(BCOL[:, :], t[:, 44:92])
                    dve.tensor_copy(FW[:, :, :], t[:, 92:92 + 3 * 44].rearrange("p (k n) -> p k n", k=3))
                    dve.tensor_copy(WST[:, :, :], t[:, 512:1024].rearrange("p (g n) -> p g n", g=4))\
                        .then_inc(drained[3], 1)
                    wait_copied(dve, s)
                elif kind == "kt" and n == 0:
                    dve.wait_ge(pool_in, POOL_IN)
                    for d in range(2):
                        for h in range(HEADS):
                            o, j = DH * (h % 2), h // 2
                            last = dve.tensor_scalar(CST[o:o + DH, d, j, 1, o:o + DH], ONES[o:o + DH, 0:DH],
                                                     SCOL[o:o + DH, 40 + 2 * d + j:41 + 2 * d + j], None, ALU.mult)
                    last.then_inc(n0_set, 1)
                elif kind == "v":
                    t = wait_filled(dve, s)
                    wait_first_reader(dve, s)
                    dve.wait_ge(later_in, NLATER)
                    gb = GB[:, :].rearrange("p (d k h) -> p d k h", d=2, k=2)
                    for b, g in enumerate(range(2 * n, min(2 * n + 2, TILES))):
                        last = dve.tensor_tensor(
                            G2[:, g, :, :].rearrange("p k (d x) -> p d k x", d=2)[:, :, :, 0:HEADS],
                            t[:, 512 * b + DG:512 * b + DG + 16].rearrange("p (d k h) -> p d k h", d=2, k=2),
                            gb, ALU.add)
                    last.then_inc(drained[USE[s][0]], 1)
                elif kind == "gf":
                    t = wait_filled(dve, s)
                    wait_first_reader(dve, s)
                    dve.tensor_scalar(NM[:, :], t[0:64, 0:TOK], 0.0, None, ALU.min).then_inc(drained[USE[s][0]], 1)
                    wait_copied(dve, s)
                    gate_rows()
                elif kind == "mx":
                    t = wait_filled(dve, s)
                    dve.tensor_tensor(SA[:, n, 0:TOK].rearrange("p (g n) -> p g n", g=TILES),
                                      t[:, 0:TOK].rearrange("p (g n) -> p g n", g=TILES),
                                      BSB[:, n:n + 1, :].to_broadcast([P, TILES, P]), ALU.add)\
                        .then_inc(drained[USE[s][0]], 1)
                elif kind == "gu":
                    t = wait_filled(dve, s)
                    wait_copied(dve, ("mx", n))
                    dve.tensor_tensor(Y[:, 2 + n, :].rearrange("p (h n) -> p h n", h=2), halves(t),
                                      SA[:, n, 0:TOK].rearrange("p (h n) -> p h n", h=2), ALU.mult)\
                        .then_inc(drained[USE[s][0]], 1)
                    if n == 1:
                        wait_copied(dve, ("gu", 0))
                        wait_copied(dve, s)
                        dve.memset(SA[:, :, :], 0.0).then_inc(pads_zero, 1)
                elif kind == "ct":
                    t = wait_filled(dve, s)
                    wait_first_reader(dve, s)
                    dve.tensor_copy(COLS[:, :, 0, :],
                                    t[:, 0:TOK].rearrange("p (g k n) -> p g k n", g=TILES, k=2)[:, :, 0, :])\
                        .then_inc(drained[USE[s][0]], 1)
                    wait_copied(dve, s)
                elif kind == "B":
                    g, d = MUNITS[n]
                    dve.wait_ge(psM_full, n + 1)
                    if n:
                        dve.wait_ge(s_ready, n)
                    for h in range(HEADS):
                        last = dve.scalar_tensor_tensor(out=XE[:, h, :], in0=psM[:, cols(h)],
                                                        scalar=COLS[:, g, 0, 32 * d + h:32 * d + h + 1],
                                                        in1=MASK[:, d, :], op0=ALU.add, op1=ALU.min)
                    last.then_inc(xe_ready, 1)
                    dve.wait_ge(we_ready, n + 1)
                    if n:
                        dve.wait_ge(psN_full, n)
                    if g:
                        dve.tensor_tensor(QW[:, :, :], QK[:, 0:2, cols(g)], WE[:, :, 0, :], ALU.mult)\
                            .then_inc(qw_ready, 1)
                    dve.wait_ge(e_ready, n + 1)
                    dve.wait_ge(psQ_full, n + 1)
                    dve.tensor_tensor(SS[:, :, :], XE[:, :, :], psQ.rearrange("p (h n) -> p h n", h=HEADS), ALU.mult)\
                        .then_inc(s_ready, 1)
                elif kind == "C":
                    g, d = MUNITS[n]
                    dve.wait_ge(psN_full, n + 1)
                    num = psN.rearrange("p (j k n) -> p j k n", j=2, k=2)
                    link(dve.scalar_tensor_tensor(out=WE[:, :, 1, :], in0=num[:, :, 1, :], scalar=-1.0,
                                                  in1=WE[:, :, 1, :], op0=ALU.mult, op1=ALU.max))
                    link(dve.tensor_tensor(WE[:, :, 1, :], num[:, :, 1, :], WE[:, :, 1, :], ALU.max))
                    link(dve.reciprocal(WE[:, :, 1, :], WE[:, :, 1, :]))
                    h_out = QW[:, :, :] if d else HA[:, :, cols(g)]
                    dve.tensor_tensor(h_out, num[:, :, 0, :], WE[:, :, 1, :], ALU.mult).then_inc(n_read, 1)
                    if d:
                        dve.wait_ge(n_read, n + 1)
                        link(dve.tensor_tensor(HA[:, :, cols(g)], HA[:, :, cols(g)], QW[:, :, :], ALU.add))
                    if (g, d) in UPD:
                        upd = psM.rearrange("p (j k n) -> p j k n", j=2, k=2)
                        dve.wait_ge(psC_full, UPD.index((g, d)) + 1)
                        t = 0 if d else P - 1
                        for h in range(HEADS):
                            o, j = DH * (h % 2), h // 2
                            r = slice(o, o + DH)
                            if g == 0:
                                dve.tensor_copy(CSO[r, d, j, :], upd[r, j, 0, o:o + DH])
                                last = dve.tensor_copy(NS[r, d, j:j + 1], upd[r, j, 1, 0:1])
                            else:
                                last = dve.scalar_tensor_tensor(out=CST[r, d, j, :, o:o + DH],
                                                                in0=CST[r, d, j, :, o:o + DH],
                                                                scalar=WE[r, j, 0, t:t + 1],
                                                                in1=upd[r, j, :, o:o + DH], op0=ALU.mult, op1=ALU.add)
                        last.then_inc(c_read, 1)
                        dve.wait_ge(c_read, UPD.index((g, d)) + 1)
                    if n == len(MUNITS) - 1:
                        output_gate(0)
                elif kind == "cx":
                    t = wait_filled(dve, s)
                    wait_copied(dve, ("cc", n))
                    for a, b, o in pieces(PC_, PS_):
                        last = dve.tensor_tensor(SA[:, 0, o:o + b - a], t[:, a:b], SA[:, 0, o:o + b - a], ALU.mult)
                    last.then_inc(drained[USE[s][0]], 1)
                    wait_copied(dve, s)
                    w = PADW - 2 * PC_
                    if n:
                        wait_copied(dve, ("cb", 0))
                    link(dve.tensor_scalar(SBb[:, 0:w], SA[:, 0, PC_ - 1:PC_ - 1 + w], SCOL[:, 32 + n:33 + n], None,
                                           ALU.mult))
                    link(dve.scalar_tensor_tensor(out=SBb[:, 0:w], in0=SA[:, 0, PC_:PC_ + w],
                                                  scalar=SCOL[:, 34 + n:35 + n], in1=SBb[:, 0:w],
                                                  op0=ALU.mult, op1=ALU.add))
                    dve.scalar_tensor_tensor(out=SBb[:, 0:w], in0=SA[:, 0, PC_ + 1:PC_ + 1 + w],
                                             scalar=SCOL[:, 36 + n:37 + n], in1=SBb[:, 0:w],
                                             op0=ALU.mult, op1=ALU.add).then_inc(conv_done, 1)
                elif kind == "cb":
                    t = wait_filled(dve, s)
                    dve.wait_ge(conv_done, n + 1)
                    y0 = 0
                    for a, b, o in pieces(0, PS_ - PC_):
                        last = dve.tensor_tensor(Y[:, 6 + n, y0:y0 + b - a], t[:, a:b], SBb[:, o:o + b - a], ALU.mult)
                        y0 += b - a
                    last.then_inc(drained[USE[s][0]], 1)
                elif kind == "pz":
                    pool_tile(n)
                elif kind == "o" and n:
                    output_gate(n)

            def output_gate(n):
                wait_copied(dve, ("o", n))
                if n == 0:
                    dve.wait_ge(states_out, 16 * 8)
                dve.tensor_tensor(Y[:, n, :], TMP[:, :], HA[:, n, :], ALU.mult).then_inc(y_made, 1)

            def pool_tile(j):
                wait_copied(dve, ("pz", j))
                z = SA[:, 1, :]
                if j:
                    dve.wait_ge(pooled, 1)
                else:
                    wait_copied(dve, ("cb", 1))
                link(dve.tensor_tensor(SBb[:, 1:PADW], z[:, 0:PADW - 1], z[:, 1:PADW], ALU.add))
                lo, hi = slice(0, 64), slice(64, P)
                a, b = 2, PADW - 1
                if j == 0:
                    link(dve.tensor_tensor(SCb[hi, a:b], SBb[hi, a - 1:b - 1], SBb[hi, a + 1:b + 1], ALU.add))
                else:
                    link(dve.tensor_tensor(SCb[:, a:b], SBb[:, a - 1:b - 1], SBb[:, a + 1:b + 1], ALU.add))
                    a, b = 4, PADW - 4
                    link(dve.tensor_tensor(SBb[:, a:b], SCb[:, a - 2:b - 2], SCb[:, a + 2:b + 2], ALU.add))
                    a, b = 8, PADW - 8
                    link(dve.tensor_tensor(SCb[hi, a:b], SBb[hi, a - 4:b - 4], SBb[hi, a + 4:b + 4], ALU.add))
                for r, t in ((lo, SBb), (hi, SCb)):
                    first, end = EDGE[r, 16 * j:16 * j + 8], EDGE[r, 16 * j + 8:16 * j + 16]
                    for o, w in ((PC_, first), (PS_, first), (PC_ + CTX - 8, end), (PADW - 16, end)):
                        last = dve.tensor_tensor(t[r, o:o + 8], t[r, o:o + 8], w, ALU.mult)
                link(last)
                for r, t in ((lo, SBb), (hi, SCb)):
                    for o, n in ((PC_, CTX), (PS_, TOK - CTX)):
                        last = dve.scalar_tensor_tensor(out=z[r, o:o + n], in0=t[r, o:o + n],
                                                        scalar=EDGE[r, 32 + j:33 + j], in1=z[r, o:o + n],
                                                        op0=ALU.mult, op1=ALU.subtract)
                last.then_inc(pooled, 1)

            def modulate(k):
                for group, a, b in ((0, 0, CTX), (1, CTX, TOK)):
                    last = dve.tensor_scalar(Y[:, k, a:b], Y[:, k, a:b], AMOD[:, 0, group, k:k + 1],
                                             MODC[:, k, group:group + 1], ALU.mult, ALU.add)
                last.then_inc(h_dve, 1)

            n_chunk_lo = [0]

            def chunks_to(n):
                while n_chunk_lo[0] < n:
                    m = n_chunk_lo[0]
                    src, w = chunk_source(m)
                    dve.wait_ge(act_hi, m + 1)
                    wait_chunk_slot(dve, m)
                    dve.tensor_tensor(ASLO[:, m % 3, 0:w], src, ASHI[:, m % 3, 0:w].bitcast(F32), ALU.subtract)\
                        .then_inc(act_lo, 1)
                    n_chunk_lo[0] += 1

            for at_, s in enumerate(PLAN):
                if at_ == len(HEAD_STEPS):
                    dve.wait_ge(mod1, 1)
                    for g in range(TILES - 2, TILES):
                        wait_copied(dve, ("xt", g))
                    modulate(1)
                    for k in range(KC):
                        if k % 2 == 0 and k + 3 < KC:
                            modulate(k + 3)
                        dve.wait_ge(h_hi, k + 1)
                        dve.tensor_tensor(Hlo[:, k, :], Y[:, k, :], Hhi[:, k, :].bitcast(F32), ALU.subtract)\
                            .then_inc(h_lo, 1)
                split_to(goal[at_])
                if s == ("o", 1):
                    chunks_to(3)
                mix(s)

            def epilogue(stage, g):
                n = TILES * (stage == "down") + g
                i = 1 + 2 * (stage == "down")
                key = (stage, "epi", g)
                t = wait_filled(dve, key)
                dve.wait_ge(y_root, n + 1)
                link(dve.reciprocal(STAT[:, i, 2, g:g + 1], STAT[:, i, 1, g:g + 1]))
                if n:
                    dve.wait_ge(x2_new, n)
                dve.scalar_tensor_tensor(out=T2[:, :], in0=t[:, :], scalar=STAT[:, i, 2, g:g + 1],
                                         in1=GATE[:, int(g > 0), :], op0=ALU.mult, op1=ALU.mult)\
                    .then_inc(drained[USE[key][0]], 1)
                wait_copied(dve, key)
                if stage == "out" and g == 0:
                    dve.wait_ge(x2_in, 16 * TILES)
                elif stage == "out":
                    dve.wait_ge(x2_pos, g)
                dve.tensor_tensor(X2[:, g, :], T2[:, :], X2[:, g, :], ALU.add).then_inc(x2_new, 1)

            for at_, s in enumerate(PLAN_OUT, len(PLAN)):
                if s[0] in ("k", "k2"):
                    chunks_to(chunk_limit("out", s))
                split_to(early_lo.get(s, goal[at_]))
                if s[0] == "epi":
                    epilogue("out", s[1])
                elif s[0] == "nrm":
                    g = s[1]
                    dve.wait_ge(n_root, g + 1)
                    link(dve.reciprocal(STAT[:, 2, 2, g:g + 1], STAT[:, 2, 1, g:g + 1]))
                    if g > 1:
                        wait_filled(dve, ("out", "tr", g - 2))
                    dve.tensor_scalar(XN2[:, g % 2, :], X2[:, g, :], STAT[:, 2, 2, g:g + 1], None, ALU.mult)\
                        .then_inc(n_xn, 1)
                elif s[0] == "tr":
                    g = s[1]
                    key = ("out",) + s
                    t = wait_filled(dve, key)
                    if g > 1:
                        dve.wait_ge(n_hi, g - 1)
                        dve.wait_ge(n_lo, g - 1)
                    for k in range(KC // 2, KC):
                        last = dve.tensor_scalar(HT2[:, g % 2, k, :], t[:, cols(k)], AMOD[:, 1, int(g > 0), k:k + 1],
                                                 MODC[:, 24 + k, int(g > 0):int(g > 0) + 1], ALU.mult, ALU.add)
                    last.then_inc(drained[USE[key][0]], 1)
                elif s[0] == "lo" and s[1] >= POOL_LO:
                    g = s[1]
                    dve.wait_ge(n_lo, g)
                    wait_copied(dve, ("out", "tr", g))
                    dve.wait_ge(n_hi, g + 1)
                    dve.tensor_tensor(Hlo[:, :, cols(g)], HT2[:, g % 2, :, :], Hhi[:, :, cols(g)].bitcast(F32), ALU.subtract)\
                        .then_inc(n_lo, 1)
                elif s[0] == "ada":
                    ada(("out",) + s, s[1])
                elif s[0] == "p2":
                    piece2(("out",) + s, s[1])

            base, per = n_link[0], 2 * RING
            split_base = splits_to[UP0 + AHEAD]
            with dve.Fori(0, LOOPS) as i:
                for s in range(RING):
                    u = UP0 + s + AHEAD
                    dve.wait_ge(hi_split, i * RING + (split_base + s + 1))
                    dve.tensor_tensor(WLO[:, u % RING, 0:D], RAW[:, u % RING, 0:D], WHI[:, u % RING, 0:D].bitcast(F32),
                                      ALU.subtract).then_inc(lo_split, 1)
                    pair, _, _, after = USE[("up", s)]
                    q, r = s // 2, s % 2
                    dve.wait_ge(drained[pair], i + after)
                    f = i * 2 + (q + FT * r)
                    if r == 0:
                        dve.wait_ge(ff_out, i * 2 + (q + 1))
                    dve.tensor_scalar(CV[:, q, r, :], UP[:, q, r, 0:AW], FW[:, 0, bass.ds(f, 1)], None, ALU.mult)\
                        .then_inc(vlink, 1)
                    for k in (1, 2):
                        dve.wait_ge(vlink, i * per + (base + 2 * s + k))
                        dve.scalar_tensor_tensor(out=CV[:, q, r, :], in0=UP[:, q, r, k:k + AW],
                                                 scalar=FW[:, k, bass.ds(f, 1)], in1=CV[:, q, r, :],
                                                 op0=ALU.mult, op1=ALU.add).then_inc(vlink if k == 1 else up_free, 1)
                    if r == 1:
                        dve.wait_ge(silu_out, i * 2 + (q + 1))
                        dve.tensor_tensor(ACTF[:, bass.ds(i * 2 + q, 1), :], CV[:, q:q + 1, 0, :], CV[:, q:q + 1, 1, :],
                                          ALU.mult).then_inc(ff_out, 1)
            n_link[0] += LOOPS * per
            split[0] += 2 * FT
            split_to(UP0 + 2 * FT + 5)

            for at_, s in enumerate(PLAN_DOWN, UP_STEP + 1):
                if s == ("ada", 11):
                    chunks_to(2 * KC + 3)
                elif s[0] in ("k", "k2"):
                    chunks_to(chunk_limit("down", s))
                split_to(goal[at_])
                if s[0] == "ada":
                    ada(("down",) + s, s[1])
                elif s[0] == "p2":
                    piece2(("down",) + s, s[1])
                elif s[0] == "epi":
                    epilogue("down", s[1])

        @block.tensor
        def _(pe):
            def ada(key, first):
                t = wait_free(pe, key)
                for q in range(4):
                    u = first + q
                    pe.wait_ge(raw_in[u % RING], raw_count(u))
                    for k in range(2):
                        last = pe.matmul(t[0:4, 0:512], COND[:, 2 * q + k, :], RAW[:, u % RING, 512 * k:512 * k + 512],
                                         start=(q == 0 and k == 0), stop=(q == 3 and k == 1))
                    last.then_inc(ada_used if q < 3 else filled[USE[key][0]], 1)

            def split_rows(s):
                t = wait_free(pe, s)
                n = len(AD_BLOCKS[s[1]])
                w, per = P * n, KC // n
                for q in range(n):
                    u = UPTO[s] - n + q
                    wait_split(pe, u)
                    for k in range(per):
                        c = 4 * (per * q + k)
                        for part in (WHI, WLO):
                            last = pe.matmul(t[:, 0:w], CONDHL[:, c:c + P], part[:, u % RING, w * k:w * k + w],
                                             start=(q == 0 and k == 0 and part is WHI),
                                             stop=(q == n - 1 and k == per - 1 and part is WLO))
                    last.then_inc(ada_used if q < n - 1 else filled[USE[s][0]], 1)

            def columns(s):
                wait_copied(pe, ("ad", s[1]))
                t = wait_free(pe, s)
                for m in range(len(AD_BLOCKS[s[1]])):
                    last = pe.matmul(t[:, 2 * m:2 * m + 2], MODROW[:, cols(m)], SELHL[:, :, 0], start=True, stop=True)
                last.then_inc(filled[USE[s][0]], 1)

            def piece2(key, row_key):
                wait_copied(pe, row_key)
                t = wait_free(pe, key)
                for group in range(2):
                    last = pe.matmul(t[:, 512 * group:512 * group + 512], SELHL[:, group, :], MODROW[:, :],
                                     start=True, stop=True)
                last.then_inc(filled[USE[key][0]], 1)

            def channel_tile(t, n_or_slot, wait_h=False, part=(0, 1)):
                for k in range(KC):
                    if wait_h:
                        pe.wait_ge(h_lo, k + 1)
                    for n, (w, h) in enumerate(((WHI, Hhi), (WHI, Hlo), (WLO, Hhi))):
                        for half in part:
                            last = pe.matmul(t[:, 512 * half:512 * half + HALF], w[:, n_or_slot, cols(k)],
                                             h[:, k, HALF * half:HALF * half + HALF],
                                             start=(k == 0 and n == 0), stop=(k == KC - 1 and n == 2))
                return last

            def token_tile(out, g, unit, w):
                for k in range(KC):
                    slot = (unit + k // 4) % RING
                    for n, (wt, h) in enumerate(((WHI, Hhi), (WHI, Hlo), (WLO, Hhi))):
                        last = pe.matmul(out, h[:, k, cols(g)], wt[:, slot, w * (k % 4):w * (k % 4) + w],
                                         start=(k == 0 and n == 0), stop=(k == KC - 1 and n == 2))
                return last

            def mix(s):
                kind, n = s
                if kind == "ada":
                    ada(s, UPTO[s] - 4)
                elif kind == "ad":
                    split_rows(s)
                elif kind == "p2":
                    piece2(s, ("ada", n))
                elif kind == "rows":
                    columns(s)
                elif kind == "consts":
                    pe.wait_ge(pool_made, 8)
                    pe.wait_ge(consts_in, NCONST)
                    t = PAIR[3]
                    pe.transpose(t[:, 0:44], SMALL[:, :], IDENT[0:44, 0:44])
                    pe.transpose(t[:, 44:92], BROWS[:, :], IDENT[0:48, 0:48])
                    for k in range(3):
                        pe.transpose(t[:, 92 + 44 * k:136 + 44 * k], FROWS[:, k, :], IDENT[0:44, 0:44])
                    for w in range(4):
                        last = pe.transpose(t[:, 512 + P * w:640 + P * w], WS[:, w, :], IDENT[:, :])
                    last.then_inc(filled[3], 1)
                elif kind == "xt":
                    pe.wait_ge(x_normed, n + 1)
                    t = wait_free(pe, s)
                    for k in range(KC):
                        last = pe.transpose(t[:, cols(k)], XN[:, n % 2, cols(k)], IDENT[:, :])
                    last.then_inc(filled[USE[s][0]], 1)
                elif kind in FEATURE:
                    u = UPTO[s] - 1
                    t = wait_free(pe, s)
                    wait_split(pe, u)
                    channel_tile(t, u % RING, s == ("q", 0)).then_inc(filled[USE[s][0]], 1)
                elif kind == "v":
                    u = UPTO[s] - 2
                    t = wait_free(pe, s)
                    wait_split(pe, u + 1)
                    for b, g in enumerate(range(2 * n, min(2 * n + 2, TILES))):
                        last = token_tile(t[:, 512 * b:512 * b + DG + 16], g, u, DG + 16)
                    last.then_inc(filled[USE[s][0]], 1)
                elif kind == "gv":
                    u = UPTO[s] - 2
                    t = wait_free(pe, s)
                    wait_split(pe, u + 1)
                    for b, g in enumerate(range(0, 4) if n == 0 else [4]):
                        last = token_tile(t[:, DG * b:DG * b + DG], g, u, DG)
                    last.then_inc(filled[USE[s][0]], 1)
                elif kind in ("gi", "gf"):
                    for v in range(3):
                        wait_copied(pe, ("v", v))
                    t = wait_free(pe, s)
                    for g in range(TILES):
                        last = pe.transpose(t[0:64, cols(g)], G2[:, g, int(kind == "gf"), :], IDENT[:, :])
                    last.then_inc(filled[USE[s][0]], 1)
                elif kind == "kt":
                    for i in range(2):
                        wait_copied(pe, ("k", i))
                    t = wait_free(pe, s)
                    for b, g in enumerate(range(0, 4) if n == 0 else [4]):
                        for j in range(2):
                            last = pe.transpose(t[:, DG * b + P * j:DG * b + P * j + P], QK[:, 2 + j, cols(g)],
                                                IDENT[:, :])
                    last.then_inc(filled[USE[s][0]], 1)
                elif kind == "mx":
                    wait_copied(pe, ("gv", 0))
                    wait_copied(pe, ("gv", 1))
                    t = wait_free(pe, s)
                    for g in range(TILES):
                        for b in range(2):
                            w = 2 * n + b
                            last = pe.matmul(t[DH * b:DH * b + DH, cols(g)], GV[:, g, DH * w:DH * w + DH], WST[:, w, :],
                                             start=True, stop=True)
                    last.then_inc(filled[USE[s][0]], 1)
                elif kind == "ct":
                    pe.wait_ge(rows_ready, 1)
                    t = wait_free(pe, s)
                    for g in range(TILES):
                        for b, src in enumerate((AR, LF)):
                            o = P * g + 64 * b
                            last = pe.transpose(t[:, o:o + 64], src[:, cols(g)], IDENT[0:64, 0:64])
                    last.then_inc(filled[USE[s][0]], 1)
                elif kind == "B":
                    g, d = MUNITS[n]
                    if n == 0:
                        for key in ("xt", 3), ("xt", 4):
                            wait_copied(pe, key)
                        wait_copied(pe, ("ct", 0))
                        for i in range(2):
                            wait_copied(pe, ("q", i))
                    if n:
                        pe.wait_ge(xe_ready, n)
                        pe.wait_ge(c_read, len([u for u in UPD if m_index[u] < n]))
                    for h in range(HEADS):
                        r = 32 * d + h
                        last = pe.matmul(psM[:, cols(h)], IDENT[0:64, r:r + 1].to_broadcast([64, P]), NM[:, cols(g)],
                                         start=True, stop=True)
                    last.then_inc(psM_full, 1)
                    if n:
                        pe.wait_ge(we_ready, n)
                    for j in range(2):
                        last = pe.matmul(psW[:, 2 * P * j:2 * P * j + 2 * P], SELP[:, 2 * d + j, :],
                                         WR[:, g, :, :].rearrange("p k n -> p (k n)"), start=True, stop=True)
                    last.then_inc(psW_full, 1)
                    if n:
                        pe.wait_ge(s_ready, n)
                    for b in range(2):
                        if b:
                            pe.wait_ge(psQ_even, n + 1)
                        r = slice(DH * b, DH * b + DH)
                        for j in range(2):
                            last = pe.matmul(psQ[:, cols(2 * j + b)], QK[r, 2 + j, cols(g)], QK[r, j, cols(g)],
                                             start=True, stop=True)
                        last.then_inc(psQ_full if b else psQ_even, 1)
                elif kind == "C":
                    g, d = MUNITS[n]
                    pe.wait_ge(s_ready, n + 1)
                    carry = g > 0
                    if carry:
                        pe.wait_ge(qw_ready, CARRY.index((g, d)) + 1)
                        pe.wait_ge(n0_set, 1)
                        pe.wait_ge(c_read, len([u for u in UPD if m_index[u] < n]))
                    if n:
                        pe.wait_ge(n_read, n)
                    for j in range(2):
                        for k in range(2):
                            o = P * (2 * j + k)
                            if carry:
                                pe.matmul(psN[:, o:o + P], CST[:, d, j, k, :], QW[:, j, :], start=True, stop=False,
                                          skip_group_check=True)
                            for b in range(2):
                                h = 2 * j + b
                                lhs = ONES[:, 0:DH] if k else V[:, g, DH * h:DH * h + DH]
                                last = pe.matmul(psN[DH * b:DH * b + DH, o:o + P], lhs, SS[:, h, :], start=not carry,
                                                 stop=True, skip_group_check=True)
                    last.then_inc(psN_full, 1)
                    if (g, d) in UPD:
                        pe.wait_ge(kw_ready, UPD.index((g, d)) + 1)
                        for j in range(2):
                            for k in range(2):
                                o = P * (2 * j + k)
                                last = pe.matmul(psM[:, o:o + P], KW[:, cols(j)], ONES[:, :] if k else V[:, g, cols(j)],
                                                 start=True, stop=True)
                        last.then_inc(psC_full, 1)
                elif kind == "pl":
                    pe.wait_ge(pooled, n + 1)
                    t = wait_free(pe, s)
                    for a, b, o in ((0, CTX, PC_), (512, 1024, PS_)):
                        last = pe.matmul(t[:, a:b], PWB[:, n, :], SA[:, 1, o:o + b - a], start=True, stop=True)
                    last.then_inc(filled[USE[s][0]], 1)

            pe.wait_ge(cond_split, 1)
            for s in PLAN:
                mix(s)

            def chunk_tile(stage, half, k, b):
                m = chunk_at[(stage, half, k)]
                u = chunk_unit[m]
                key = (stage, "epi", PASS_TILES[half][b])
                t = PAIR[USE[key][0]]
                if b == 0:
                    wait_split(pe, u)
                    pe.wait_ge(act_lo, m + 1)
                if k == 0:
                    wait_free(pe, key)
                last_k = (KC if stage == "out" else FT) - 1
                o = P * b + (2 if stage == "down" and half == 0 and b else 0)
                for n, (a, w) in enumerate(((ASHI, WHI), (ASLO, WHI), (ASHI, WLO))):
                    for c0 in (0, 512):
                        last = pe.matmul(t[:, c0:c0 + 512], a[:, m % 3, o:o + P], w[:, u % RING, c0:c0 + 512],
                                         start=(k == 0 and n == 0), stop=(k == last_k and n == 2))
                if k == last_k:
                    last.then_inc(filled[USE[key][0]], 1)
                return last

            def chunks(stage, s):
                tiles = range(len(PASS_TILES[s[1]]))
                if s[0] == "k":
                    for b in tiles:
                        last = chunk_tile(stage, s[1], s[2], b)
                    last.then_inc(chunk_used, 1)
                else:
                    for b in tiles:
                        for k in k_chunks(s):
                            chunk_tile(stage, s[1], k, b)

            pe.wait_ge(n_read, len(MUNITS))
            for s in PLAN_OUT:
                if s[0] in ("k", "k2"):
                    chunks("out", s)
                elif s[0] == "tr":
                    g = s[1]
                    key = ("out",) + s
                    t = wait_free(pe, key)
                    pe.wait_ge(n_xn, g + 1)
                    for k in range(KC):
                        last = pe.transpose(t[:, cols(k)], XN2[:, g % 2, cols(k)], IDENT[:, :])
                    last.then_inc(filled[USE[key][0]], 1)
                elif s[0] == "ada":
                    ada(("out",) + s, UPTO[("out",) + s] - 4)
                elif s[0] == "p2":
                    piece2(("out",) + s, ("out", "ada", s[1]))

            for half in range(2):
                pe.wait_ge(n_lo, (3, TILES)[half])
                for s in range(2):
                    if half == 0:
                        wait_split(pe, UP0 + s)
                        pe.wait_ge(drained[s], USE[("up", s)][2])
                    last = channel_tile(PAIR[s], s, part=(half,))
                    if half == 1:
                        last.then_inc(filled[s], 1)
            for s in range(2, RING):
                wait_split(pe, UP0 + s)
                pe.wait_ge(drained[s], USE[("up", s)][2])
                channel_tile(PAIR[s], s).then_inc(filled[s], 1)
            with pe.Fori(1, LOOPS) as i:
                for s in range(RING):
                    pair, _, before, _ = USE[("up", s)]
                    pe.wait_ge(lo_split, i * RING + (splits_to[UP0] + s + 1))
                    pe.wait_ge(drained[pair], i + before)
                    channel_tile(PAIR[pair], s).then_inc(filled[pair], 1)
            for s in PLAN_DOWN:
                if s[0] in ("k", "k2"):
                    chunks("down", s)
                elif s[0] == "ada":
                    ada(("down",) + s, UPTO[("down",) + s] - 4)
                elif s[0] == "p2":
                    piece2(("down",) + s, ("down", "ada", s[1]))


_INS = ["x_prompt", "x_sample", "state_C", "state_n", "state_m", "c", "c_ctx", "norm_g", "ada_w", "ada_b", "w_in",
        "gate_b", "gmlp_ws", "gmlp_b", "pool_w", "pool_scale", "conv_w", "w_out", "ffn_up", "ffn_conv", "ffn_down"]
_OUTS = [(1, 128, 1024), (1, 512, 1024), (1, 1, 2, 4, 64, 64), (1, 1, 2, 4, 64), (1, 1, 2, 4)]


def _shape_tables():
    import numpy as np
    quarter = D // 4
    omega = (1.0 / (10000.0 ** (np.arange(quarter, dtype=np.float32) / np.float32(quarter)))).astype(np.float32)

    def emb(n):
        a = np.arange(n, dtype=np.float32)[:, None] * omega[None, :]
        return np.concatenate([np.sin(a), np.cos(a)], axis=-1).astype(np.float32)

    grid_w = 64
    rows = emb((TOK - CTX) // grid_w)
    edge = np.ones((P, 34), np.float32)
    for j in range(2):
        for half in range(2):
            w = 2 ** (2 * j + half + 1)
            r = slice(64 * half, 64 * half + 64)
            t = np.arange(8)
            edge[r, 16 * j:16 * j + 8] = w / (np.minimum(t, w // 2) + w // 2)
            back = 8 - t
            edge[r, 16 * j + 8:16 * j + 16] = w / (np.minimum(back, w // 2) + w // 2)
            edge[r, 32 + j] = 1.0 / w
    return {"pos_row": np.ascontiguousarray(rows.reshape(TILES - 1, 2, 512).transpose(1, 0, 2)),
            "pos_col": emb(grid_w), "pool_edge": edge}


def kernel(**inputs):
    import numpy as _np
    import concourse.bacc as _bacc
    from concourse import mybir as _mybir
    from concourse.bass_utils import run_bass_kernel_spmd as _run

    nc = _bacc.Bacc("TRN2", target_bir_lowering=False, num_devices=1)
    tables = _shape_tables()
    arrays, args = {}, []
    for name in _INS + list(tables):
        a = _np.ascontiguousarray(inputs[name] if name in inputs else tables[name])
        arrays[f"in_{name}_dram"] = a
        args.append(nc.dram_tensor(f"in_{name}_dram", a.shape, _mybir.dt.from_np(a.dtype), kind="ExternalInput").ap())
    for i, shape in enumerate(_OUTS):
        args.append(nc.dram_tensor(f"out_{i}_dram", shape, _mybir.dt.float32, kind="ExternalOutput").ap())
    hybrid_trunk_layer(nc, *args)
    r = _run(nc, [arrays], core_ids=[0])
    return tuple(r.results[0][f"out_{i}_dram"] for i in range(len(_OUTS)))
```
